# Optimizing a Trainium2 kernel written in Bass

```python
import jax, jax.numpy as jnp
from jax import lax
import numpy as np

D_MODEL = 1024
BATCH = 1
SEQ = 256
DEPTH = 4

MIXER_ORDER = ('dsa', 'moba', 'retention')
N_MIXERS = 3
ROPE_THETA = 10000.0
ALPHA = (2 * DEPTH) ** 0.25
BETA = (8 * DEPTH) ** -0.25
LN_EPS = 1e-5
GN_EPS = 1e-6
NEG_INF = -1e30

DSA_HEADS = 16
DSA_HEAD_DIM = D_MODEL // DSA_HEADS
IDX_HEADS = 8
IDX_DIM = 64
DSA_TOPK = 256
DSA_Q_BLOCK = 128

MOBA_HEADS = 16
MOBA_HEAD_DIM = D_MODEL // MOBA_HEADS
MOBA_BLOCK = 256
MOBA_TOPK = 3
MOBA_Q_CHUNK = 32

RET_HEADS = 4
RET_QK_DIM = D_MODEL // RET_HEADS
RET_V_DIM = 2 * RET_QK_DIM
RET_CHUNK = 128

D_FF = 2816
CONV_WIDTH = 3

kernel_name = 'hybrid_dsa_moba_retention_deepnorm'

def _rope_cos_sin(seq_len, dim):
    inv = 1.0 / (ROPE_THETA ** (jnp.arange(0, dim, 2, dtype=jnp.float32) / dim))
    ang = jnp.arange(seq_len, dtype=jnp.float32)[:, None] * inv[None, :]
    return jnp.cos(ang), jnp.sin(ang)

def _apply_rope(x, cos, sin):
    half = x.shape[-1] // 2
    xf = x.astype(jnp.float32)
    x1, x2 = xf[..., :half], xf[..., half:]
    c, s = cos[:, None, :], sin[:, None, :]
    return jnp.concatenate([x1 * c - x2 * s, x1 * s + x2 * c], axis=-1).astype(x.dtype)

def _layer_norm(x, g, b):
    xf = x.astype(jnp.float32)
    mu = jnp.mean(xf, axis=-1, keepdims=True)
    var = jnp.mean(jnp.square(xf - mu), axis=-1, keepdims=True)
    return ((xf - mu) * lax.rsqrt(var + LN_EPS) * g + b).astype(x.dtype)

def _dsa_mixer(x, w_in, w_out):
    bsz, seq, _ = x.shape
    h, dh, hi, di = DSA_HEADS, DSA_HEAD_DIM, IDX_HEADS, IDX_DIM
    sizes = [h * dh, dh, dh, hi * di, di, hi]
    offs = np.cumsum(sizes)[:-1].tolist()
    q, k, v, qi, ki, wi = jnp.split(x @ w_in, offs, axis=-1)
    cos, sin = _rope_cos_sin(seq, dh)
    ci, si = _rope_cos_sin(seq, di)
    q = _apply_rope(q.reshape(bsz, seq, h, dh), cos, sin)
    k = _apply_rope(k.reshape(bsz, seq, 1, dh), cos, sin)[:, :, 0]
    qi = _apply_rope(qi.reshape(bsz, seq, hi, di), ci, si)
    ki = _apply_rope(ki.reshape(bsz, seq, 1, di), ci, si)[:, :, 0]
    wi = wi * (hi ** -0.5 * di ** -0.5)
    topk = min(DSA_TOPK, seq // 4)
    nblk = seq // DSA_Q_BLOCK
    key_pos = jnp.arange(seq)
    gather_rows = jax.vmap(lambda tab, idx: tab[idx])
    scale = dh ** -0.5

    def to_blocks(t):
        return t.reshape((bsz, nblk, DSA_Q_BLOCK) + t.shape[2:]).swapaxes(0, 1)

    def block(args):
        qb, qib, wib, qpos = args
        causal = key_pos[None, :] <= qpos[:, None]
        logits = jnp.einsum('bqhd,bsd->bqhs', qib, ki).astype(jnp.float32)
        index = jnp.einsum('bqh,bqhs->bqs', wib.astype(jnp.float32), jax.nn.relu(logits))
        index = jnp.where(causal[None], index, NEG_INF)
        _, sel = lax.top_k(index, topk)
        k_sel = gather_rows(k, sel)
        v_sel = gather_rows(v, sel)
        s = jnp.einsum('bqhd,bqkd->bqhk', qb, k_sel).astype(jnp.float32) * scale
        valid = sel <= qpos[None, :, None]
        p = jax.nn.softmax(jnp.where(valid[:, :, None, :], s, NEG_INF), axis=-1)
        return jnp.einsum('bqhk,bqkd->bqhd', p.astype(v.dtype), v_sel)

    qpos_b = jnp.arange(seq).reshape(nblk, DSA_Q_BLOCK)
    o = lax.map(block, (to_blocks(q), to_blocks(qi), to_blocks(wi), qpos_b))
    o = o.swapaxes(0, 1).reshape(bsz, seq, h * dh)
    return o @ w_out

def _moba_mixer(x, w_in, w_out):
    bsz, seq, _ = x.shape
    h, dh, blk, qc_len = MOBA_HEADS, MOBA_HEAD_DIM, MOBA_BLOCK, MOBA_Q_CHUNK
    q, k, v = jnp.split(x @ w_in, 3, axis=-1)
    cos, sin = _rope_cos_sin(seq, dh)
    q = _apply_rope(q.reshape(bsz, seq, h, dh), cos, sin)
    k = _apply_rope(k.reshape(bsz, seq, h, dh), cos, sin)
    v = v.reshape(bsz, seq, h, dh)
    n_kb = -(-seq // blk)
    pad = n_kb * blk - seq
    padw = ((0, 0), (0, pad), (0, 0), (0, 0))
    k_blocks = jnp.pad(k, padw).reshape(bsz, n_kb, blk, h, dh).transpose(0, 3, 1, 2, 4)
    v_blocks = jnp.pad(v, padw).reshape(bsz, n_kb, blk, h, dh).transpose(0, 3, 1, 2, 4)
    k_mean = jnp.mean(k_blocks.astype(jnp.float32), axis=3)
    n_sel = min(MOBA_TOPK, n_kb - 1)
    n_chunk = seq // qc_len
    scale = dh ** -0.5
    b_ix = jnp.arange(bsz)[:, None, None, None]
    h_ix = jnp.arange(h)[None, None, :, None]
    blk_ids = jnp.arange(n_kb)

    def chunk(args):
        qc, c = args
        start = c * qc_len
        own = start // blk
        qpos = start + jnp.arange(qc_len)
        k_own = lax.dynamic_index_in_dim(k_blocks, own, axis=2, keepdims=False)
        v_own = lax.dynamic_index_in_dim(v_blocks, own, axis=2, keepdims=False)
        own_pos = own * blk + jnp.arange(blk)
        s_own = jnp.einsum('bqhd,bhsd->bhqs', qc, k_own).astype(jnp.float32) * scale
        s_own = jnp.where((own_pos[None, :] <= qpos[:, None])[None, None], s_own, NEG_INF)
        if n_sel == 0:
            p = jax.nn.softmax(s_own, axis=-1).astype(v.dtype)
            return jnp.einsum('bhqs,bhsd->bqhd', p, v_own)
        gate = jnp.einsum('bqhd,bhnd->bqhn', qc.astype(jnp.float32), k_mean)
        gate = jnp.where(blk_ids < own, gate, NEG_INF)
        _, sel = lax.top_k(gate, n_sel)
        valid = sel < own
        k_sel = k_blocks[b_ix, h_ix, sel]
        v_sel = v_blocks[b_ix, h_ix, sel]
        s_sel = jnp.einsum('bqhd,bqhjsd->bhqjs', qc, k_sel).astype(jnp.float32) * scale
        s_sel = jnp.where(valid.transpose(0, 2, 1, 3)[..., None], s_sel, NEG_INF)
        scores = jnp.concatenate([s_sel.reshape(bsz, h, qc_len, n_sel * blk), s_own], axis=-1)
        p = jax.nn.softmax(scores, axis=-1).astype(v.dtype)
        p_sel = p[..., :n_sel * blk].reshape(bsz, h, qc_len, n_sel, blk)
        p_own = p[..., n_sel * blk:]
        return (jnp.einsum('bhqjs,bqhjsd->bqhd', p_sel, v_sel)
                + jnp.einsum('bhqs,bhsd->bqhd', p_own, v_own))

    q_chunks = q.reshape(bsz, n_chunk, qc_len, h, dh).swapaxes(0, 1)
    o = lax.map(chunk, (q_chunks, jnp.arange(n_chunk)))
    o = o.swapaxes(0, 1).reshape(bsz, seq, h * dh)
    return o @ w_out

def _retention_mixer(x, w_in, gn_g, gn_b, w_out):
    bsz, seq, _ = x.shape
    h, dk, dv, C = RET_HEADS, RET_QK_DIM, RET_V_DIM, RET_CHUNK
    q, k, v, g = jnp.split(x @ w_in, [h * dk, 2 * h * dk, 2 * h * dk + h * dv], axis=-1)
    cos, sin = _rope_cos_sin(seq, dk)
    q = _apply_rope(q.reshape(bsz, seq, h, dk), cos, sin)
    k = _apply_rope(k.reshape(bsz, seq, h, dk), cos, sin) * (dk ** -0.5)
    v = v.reshape(bsz, seq, h, dv)
    log_gamma = jnp.log1p(-(2.0 ** (-5.0 - jnp.arange(h, dtype=jnp.float32))))
    pos = jnp.arange(C, dtype=jnp.float32)
    rel = pos[:, None] - pos[None, :]
    decay = jnp.where(rel[None] >= 0,
                      jnp.exp(jnp.maximum(rel, 0.0)[None] * log_gamma[:, None, None]), 0.0)
    q_decay = jnp.exp((pos + 1.0)[None, :] * log_gamma[:, None])
    k_decay = jnp.exp((C - 1.0 - pos)[None, :] * log_gamma[:, None])
    chunk_decay = jnp.exp(C * log_gamma)
    n_c = seq // C

    def to_chunks(t):
        return t.astype(jnp.float32).reshape(bsz, n_c, C, h, t.shape[-1]).transpose(1, 0, 3, 2, 4)

    def step(state, inp):
        qc, kc, vc = inp
        inner = jnp.einsum('bhij,bhje->bhie', jnp.einsum('bhid,bhjd->bhij', qc, kc) * decay, vc)
        cross = jnp.einsum('bhid,bhde->bhie', qc, state) * q_decay[None, :, :, None]
        state = (state * chunk_decay[None, :, None, None]
                 + jnp.einsum('bhjd,bhje->bhde', kc, vc * k_decay[None, :, :, None]))
        return state, inner + cross

    state0 = jnp.zeros((bsz, h, dk, dv), jnp.float32)
    _, o = lax.scan(step, state0, (to_chunks(q), to_chunks(k), to_chunks(v)))
    o = o.transpose(1, 0, 3, 2, 4).reshape(bsz, seq, h, dv)
    mu = jnp.mean(o, axis=-1, keepdims=True)
    var = jnp.mean(jnp.square(o - mu), axis=-1, keepdims=True)
    o = ((o - mu) * lax.rsqrt(var + GN_EPS)).reshape(bsz, seq, h * dv) * gn_g + gn_b
    y = (jax.nn.silu(g.astype(jnp.float32)) * o).astype(x.dtype)
    return y @ w_out

def _conv_ffn(x, w_up, conv_w, conv_b, w_down):
    hdn = x @ w_up
    ch = hdn.shape[-1]
    hdn = lax.conv_general_dilated(
        hdn, conv_w[:, None, :].astype(hdn.dtype), window_strides=(1,),
        padding=[(CONV_WIDTH - 1, 0)], dimension_numbers=('NWC', 'WIO', 'NWC'),
        feature_group_count=ch) + conv_b
    gate, up = jnp.split(hdn, 2, axis=-1)
    return (jax.nn.silu(gate) * up) @ w_down

def _normal(key, shape, scale):
    return jax.random.normal(key, shape, jnp.float32) * scale

def _layer_params(key, i, kind):
    ks = jax.random.split(key, 12)
    p = 'l%d_' % i
    if kind == 'dsa':
        widths = (DSA_HEADS * DSA_HEAD_DIM, DSA_HEAD_DIM, DSA_HEAD_DIM, IDX_HEADS * IDX_DIM, IDX_DIM, IDX_HEADS)
        out_in = DSA_HEADS * DSA_HEAD_DIM
    elif kind == 'moba':
        widths = (MOBA_HEADS * MOBA_HEAD_DIM,) * 3
        out_in = MOBA_HEADS * MOBA_HEAD_DIM
    else:
        widths = (RET_HEADS * RET_QK_DIM, RET_HEADS * RET_QK_DIM, RET_HEADS * RET_V_DIM, RET_HEADS * RET_V_DIM)
        out_in = RET_HEADS * RET_V_DIM
    col_scale = jnp.concatenate([jnp.full((w,), BETA if j == 2 else 1.0, jnp.float32)
                                 for j, w in enumerate(widths)])
    d = {}
    d[p + 'w_in'] = _normal(ks[0], (D_MODEL, sum(widths)), D_MODEL ** -0.5) * col_scale
    if kind == 'retention':
        d[p + 'gn_g'] = 1.0 + _normal(ks[1], (RET_HEADS * RET_V_DIM,), 0.02)
        d[p + 'gn_b'] = _normal(ks[2], (RET_HEADS * RET_V_DIM,), 0.02)
    d[p + 'w_out'] = _normal(ks[3], (out_in, D_MODEL), out_in ** -0.5 * BETA)
    d[p + 'ln1_g'] = 1.0 + _normal(ks[4], (D_MODEL,), 0.02)
    d[p + 'ln1_b'] = _normal(ks[5], (D_MODEL,), 0.02)
    d[p + 'w_up'] = _normal(ks[6], (D_MODEL, 2 * D_FF), D_MODEL ** -0.5 * BETA)
    d[p + 'conv_w'] = _normal(ks[7], (CONV_WIDTH, 2 * D_FF), CONV_WIDTH ** -0.5)
    d[p + 'conv_b'] = _normal(ks[8], (2 * D_FF,), 0.02)
    d[p + 'w_down'] = _normal(ks[9], (D_FF, D_MODEL), D_FF ** -0.5 * BETA)
    d[p + 'ln2_g'] = 1.0 + _normal(ks[10], (D_MODEL,), 0.02)
    d[p + 'ln2_b'] = _normal(ks[11], (D_MODEL,), 0.02)
    return d

def setup_inputs(seed: int = 0) -> dict:
    key = jax.random.key(seed)
    keys = jax.random.split(key, 1 + DEPTH)
    params = {'x': jax.random.normal(keys[0], (BATCH, SEQ, D_MODEL), jnp.float32)}
    for i in range(DEPTH):
        params.update(_layer_params(keys[1 + i], i, MIXER_ORDER[i % N_MIXERS]))
    return params

def reference(x,
              l0_w_in, l0_w_out, l0_ln1_g, l0_ln1_b, l0_w_up, l0_conv_w, l0_conv_b, l0_w_down, l0_ln2_g, l0_ln2_b,
              l1_w_in, l1_w_out, l1_ln1_g, l1_ln1_b, l1_w_up, l1_conv_w, l1_conv_b, l1_w_down, l1_ln2_g, l1_ln2_b,
              l2_w_in, l2_gn_g, l2_gn_b, l2_w_out, l2_ln1_g, l2_ln1_b, l2_w_up, l2_conv_w, l2_conv_b, l2_w_down, l2_ln2_g, l2_ln2_b,
              l3_w_in, l3_w_out, l3_ln1_g, l3_ln1_b, l3_w_up, l3_conv_w, l3_conv_b, l3_w_down, l3_ln2_g, l3_ln2_b):
    layers = (
        ((l0_w_in, l0_w_out), (l0_ln1_g, l0_ln1_b), (l0_w_up, l0_conv_w, l0_conv_b, l0_w_down), (l0_ln2_g, l0_ln2_b)),
        ((l1_w_in, l1_w_out), (l1_ln1_g, l1_ln1_b), (l1_w_up, l1_conv_w, l1_conv_b, l1_w_down), (l1_ln2_g, l1_ln2_b)),
        ((l2_w_in, l2_gn_g, l2_gn_b, l2_w_out), (l2_ln1_g, l2_ln1_b), (l2_w_up, l2_conv_w, l2_conv_b, l2_w_down), (l2_ln2_g, l2_ln2_b)),
        ((l3_w_in, l3_w_out), (l3_ln1_g, l3_ln1_b), (l3_w_up, l3_conv_w, l3_conv_b, l3_w_down), (l3_ln2_g, l3_ln2_b)),
    )
    mixer_fns = {'dsa': _dsa_mixer, 'moba': _moba_mixer, 'retention': _retention_mixer}
    for i in range(DEPTH):
        mix_p, ln1, ffn_p, ln2 = layers[i]
        mixer = mixer_fns[MIXER_ORDER[i % N_MIXERS]]
        x = _layer_norm(ALPHA * x + mixer(x, *mix_p), *ln1)
        x = _layer_norm(ALPHA * x + _conv_ffn(x, *ffn_p), *ln2)
    return x


_drawn_inputs = setup_inputs


def setup_inputs(seed=0):
    import zlib

    import numpy as np

    out = dict(_drawn_inputs(seed))
    spreads = {}
    factors = {'l0_conv_b': 8.0,
     'l0_ln2_g': 2.77,
     'l1_ln1_g': 2.827,
     'l1_ln1_b': 2.705,
     'l1_conv_b': 8.0,
     'l1_ln2_g': 2.781,
     'l1_ln2_b': 2.695,
     'l2_gn_g': 8.0,
     'l2_gn_b': 8.0,
     'l2_ln1_g': 2.719,
     'l2_ln1_b': 2.724,
     'l2_conv_b': 21.882,
     'l2_ln2_g': 3.025,
     'l2_ln2_b': 2.765,
     'l3_ln1_g': 24.648,
     'l3_ln1_b': 23.668,
     'l3_conv_b': 30.152,
     'l3_ln2_g': 25.569,
     'l3_ln2_b': 24.333,
     'l0_ln2_b': 3.068}
    for name, (base, spread) in spreads.items():
        noise = np.random.default_rng([zlib.crc32(name.encode()), seed]).standard_normal(out[name].shape)
        drawn = base * np.exp(spread * noise) if base else spread * noise
        out[name] = __import__('jax').numpy.asarray(drawn.astype(out[name].dtype))
    for name, factor in factors.items():
        out[name] = (out[name] * factor).astype(out[name].dtype)
    return out
```

```python
from contextlib import ExitStack

import numpy as np

import concourse.bass as bass
from concourse import mybir

F32 = mybir.dt.float32
F32R = mybir.dt.float32r
ALU = mybir.AluOpType
ACT = mybir.ActivationFunctionType
AX_X = mybir.AxisListType.X

P = 128
SEQ = 256
TT = SEQ // P
D = 1024
KD = D // P
DEPTH = 4
ALPHA = (2 * DEPTH) ** 0.25
LN_EPS = 1e-5
GN_EPS = 1e-6
NEG = -1e30
TAKEN = -3e38
D_FF = 2816
STEPS = D_FF // 256
HEAD_DIM = 64
SCALE = HEAD_DIM ** -0.5
GROUPS = 4
TOPK = min(256, SEQ // 4)
IDX_HEADS = 8
IDX_SCALE = IDX_HEADS ** -0.5 * 64 ** -0.5
RET_HEADS = 4
SLOT = 2048
HALVES = 512
RING = 6
RAW = 3
TURNS = 4
MIXERS = ("dsa", "moba", "ret", "dsa")
TABLE = 1536


def plan_sublayers():
    subs = []
    slot = turn = pair = 0

    def stage(out, name, g=0, slots=0, turns=0, pairs=0):
        nonlocal slot, turn, pair
        out.append((name, g, slot, turn, pair))
        slot += slots
        turn += turns
        pair += pairs

    for kind in MIXERS:
        s = []
        stage(s, "xT", 0, 0, 4)
        if kind == "dsa":
            stage(s, "misc", 0, 1, 2)
            stage(s, "spread", 0, 0, 2)
            stage(s, "qi", 0, 1, 1)
            stage(s, "qi", 1, 1, 1)
            stage(s, "index", 0, 0, 3)
            stage(s, "index", 1, 0, 3)
            for g in range(GROUPS):
                stage(s, "q", g, 1, 1)
                stage(s, "topk", g)
            for g in range(GROUPS):
                stage(s, "scores", g, 0, 3)
                if g:
                    stage(s, "out", g - 1, 1)
                stage(s, "probsT", g, 0, 3)
                stage(s, "values", g, 0, 1, 1)
            stage(s, "out", GROUPS - 1, 1)
        elif kind == "moba":
            stage(s, "mask")
            for n in "qkv":
                stage(s, n, 0, 1, 1)
            for g in range(GROUPS):
                stage(s, "scores", g, 0, 3)
                if g:
                    stage(s, "out", g - 1, 1)
                if g + 1 < GROUPS:
                    for n in "qkv":
                        stage(s, n, g + 1, 1, 1)
                stage(s, "probsT", g, 0, 3)
                stage(s, "values", g, 0, 1, 1)
            stage(s, "out", GROUPS - 1, 1)
        else:
            stage(s, "q", 0, 1, 1)
            stage(s, "k", 0, 1, 1)
            for h in range(RET_HEADS):
                stage(s, "rv", 2 * h, 1, 1)
                stage(s, "rv", 2 * h + 1, 1, 1)
                stage(s, "rscores", h, 0, 1)
                if h:
                    stage(s, "out", 2 * h - 2, 1)
                    stage(s, "out", 2 * h - 1, 1)
                stage(s, "rgate", 2 * h, 1, 1)
                stage(s, "rgate", 2 * h + 1, 1, 1)
                stage(s, "rvalues", h, 0, 2)
                if h + 1 < RET_HEADS:
                    stage(s, "q", h + 1, 1, 1)
                    stage(s, "k", h + 1, 1, 1)
                stage(s, "ryT", h, 0, 2, 2)
            stage(s, "out", 2 * RET_HEADS - 2, 1)
            stage(s, "out", 2 * RET_HEADS - 1, 1)
        subs.append((kind, s))
        f = []
        stage(f, "xT", 0, 0, 4)
        stage(f, "ffn", 0, 3 * STEPS, 2 * STEPS, STEPS)
        subs.append(("ffn", f))
    return subs, slot, turn, pair


SUBS, N_SLOTS, N_TURNS, N_PAIRS = plan_sublayers()


def ffn_slots(first, s):
    up = first if s == 0 else first + 3 * s - 1
    return up, up + 1, first + 3 * s + (4 if s + 1 < STEPS else 2)


def lay_slots(w):
    out = np.zeros((N_SLOTS, P, SLOT), np.float32)

    def up(n, m):
        out[n].reshape(P, KD, 256)[:, :, :m.shape[1]] = m.reshape(KD, P, -1).transpose(1, 0, 2)

    def down(n, m):
        out[n] = m.reshape(2, P, D).transpose(1, 0, 2).reshape(P, SLOT)

    def halves(first, heads=4):
        c = first + np.arange(heads * HEAD_DIM).reshape(heads, 2, HEAD_DIM // 2)
        return c.transpose(1, 0, 2).ravel()

    for i, kind in enumerate(MIXERS):
        w_in, w_out = w[f"l{i}_w_in"], w[f"l{i}_w_out"]
        seen = {}
        for name, g, n, _, _ in SUBS[2 * i][1]:
            if name == "out":
                down(n, w_out[256 * g:256 * g + 256])
            elif kind == "dsa" and name == "misc":
                up(n, w_in[:, np.r_[1024:1088, 1664:1728, 1088:1152, 1728:1736]])
            elif kind == "dsa" and name == "qi":
                up(n, w_in[:, halves(1152 + 256 * g)])
            elif kind in ("dsa", "moba") and name in ("q", "k"):
                up(n, w_in[:, halves((0 if name == "q" else D) + 256 * g)])
            elif kind == "moba" and name == "v":
                up(n, w_in[:, 2 * D + 256 * g:2 * D + 256 * g + 256])
            elif kind == "ret" and name in ("q", "k", "rv", "rgate"):
                c = {"q": 0, "k": D, "rv": 2 * D, "rgate": 4 * D}[name] + 256 * g
                up(n, w_in[:, c:c + 256])
        first = SUBS[2 * i + 1][1][1][2]
        w_up, w_down = w[f"l{i}_w_up"], w[f"l{i}_w_down"]
        for s in range(STEPS):
            a, b, c = ffn_slots(first, s)
            up(a, w_up[:, 256 * s:256 * s + 256])
            up(b, w_up[:, D_FF + 256 * s:D_FF + 256 * s + 256])
            down(c, w_down[256 * s:256 * s + 256])
    return out


def lay_tables():
    def rope(dim):
        inv = (1.0 / (np.float32(10000.0) ** (np.arange(0, dim, 2, dtype=np.float32) / np.float32(dim)))).astype(np.float32)
        ang = (np.arange(SEQ, dtype=np.float32)[None, :] * inv[:, None]).astype(np.float32)
        rep = P // (dim // 2)
        return np.tile(np.cos(ang), (rep, 1)), np.tile(np.sin(ang), (rep, 1))

    att = np.zeros((P, TABLE), np.float32)
    att[:, 0:256], att[:, 256:512] = rope(HEAD_DIM)
    for j in range(4):
        for r in range(P):
            att[32 * j + r % 32, 512 + P * j + r] = 1.0
    ret = np.zeros((P, TABLE), np.float32)
    ret[:, 0:256], ret[:, 256:512] = rope(2 * P)
    key, query = np.arange(P)[:, None], np.arange(P)[None, :]
    for h in range(RET_HEADS):
        log_gamma = np.log1p(-(2.0 ** (-5.0 - h)))
        diag = np.where(query >= key, np.exp((query - key) * log_gamma), 0.0)
        across = np.exp((P + query - key) * log_gamma)
        ret[:, 512 + 256 * h:640 + 256 * h] = diag / 16
        ret[:, 640 + 256 * h:768 + 256 * h] = across / 16
    ident = np.eye(P, dtype=np.float32)
    causal = np.zeros((P, 3 * P), np.float32)
    late = np.where(np.arange(P)[None, :] > np.arange(P)[:, None], np.float32(NEG), np.float32(0))
    causal[:, 0:P] = late
    causal[:, 2 * P:3 * P] = late
    return np.stack([att, ret]), np.concatenate([ident, causal], axis=1)


def build(nc, x_in, w_slots, ln_rows, conv_cols, gn_cols, tables, consts, out, n_subs=2 * DEPTH):
    n_slots = N_SLOTS if n_subs == 2 * DEPTH else SUBS[n_subs][1][0][2]

    with ExitStack() as ctx:
        def sb(name, shape, dt=F32):
            return ctx.enter_context(nc.sbuf_tensor(name, shape, dt))

        def sem(name):
            return ctx.enter_context(nc.semaphore(name))

        raw = sb("raw", [P, RAW, SLOT])
        w_hi = sb("w_hi", [P, RING, SLOT], F32R)
        w_lo = sb("w_lo", [P, RING, SLOT], F32R)
        xT_hi = sb("xT_hi", [P, KD, SEQ], F32R)
        xT_lo = sb("xT_lo", [P, KD, SEQ], F32R)
        x = sb("x", [P, TT, D])
        ln = sb("ln", [P, 2, D])
        act_hi = sb("act_hi", [P, 2, 2, SEQ], F32R)
        act_lo = sb("act_lo", [P, 2, 2, SEQ], F32R)
        mask_r = sb("mask_r", [P, 3 * P], F32R)
        ident_r = sb("ident_r", [P, P], F32R)
        table = sb("table", [P, TABLE])
        const = sb("const", [P, 4 * P])
        conv = sb("conv", [P, 2 * D_FF // P, 4])
        gn = sb("gn", [P, 16, 2])
        stat = sb("stat", [P, 96])
        scratch = sb("scratch", [P, 9216])

        ident = const[:, 0:P]
        causal = const[:, P:4 * P]
        cos = table[:, 0:SEQ]
        sin = table[:, SEQ:2 * SEQ]

        def piece(at, *shape):
            size = int(np.prod(shape))
            v = scratch[:, at:at + size]
            if len(shape) == 2:
                return v.rearrange("p (a b) -> p a b", b=shape[1])
            if len(shape) == 3:
                return v.rearrange("p (a b c) -> p a b c", b=shape[1], c=shape[2])
            return v

        taps = [[piece(1024 * b + 512 * u, 2, SEQ) for u in range(2)] for b in range(2)]
        gate = [piece(2048 + 512 * b, 2, SEQ) for b in range(2)]
        prod = [piece(3072 + 512 * b, 2, SEQ) for b in range(2)]
        by_cos = piece(0, 2, SEQ)
        by_sin = piece(512, 2, SEQ)
        qT = [piece(1024 + 512 * g, 2, SEQ) for g in range(4)]
        k_diag = piece(3072, 2, 4, SEQ)
        v = [piece(5120 + 512 * g, TT, 256) for g in range(2)]
        probs = piece(6144, 1536)
        probsT = piece(7680, 1536)
        ki_diag = piece(6144, 2, 4, SEQ)
        relu = [piece(1024, 512), piece(1536, 512), piece(5632, 512)]
        index = piece(8192, 3 * P)
        left = piece(8576, 3 * P)
        narrow = piece(8960, SEQ)
        kT = [piece(3072 + 512 * g, 2, SEQ) for g in range(2)]
        ret_v = piece(4096, TT, 512)
        ret_gate = piece(5120, 4, SEQ)
        decayed = piece(6144, 3 * P)
        normed = piece(6656, TT, 512)
        scaled = [piece(2048 + 512 * b, 2, SEQ) for b in range(2)]
        ret_prod = [piece(7680 + 512 * b, 2, SEQ) for b in range(2)]

        acc = ctx.enter_context(nc.psum_tensor("acc", [P, TT, D], F32))
        work = ctx.enter_context(nc.psum_tensor("work", [P, TURNS, 512], F32))

        consts_in = sem("consts_in")
        gn_in = sem("gn_in")
        x_in_sem = sem("x_in_sem")
        conv_in = sem("conv_in")
        ln_in = sem("ln_in")
        table_in = sem("table_in")
        raw_in = [sem(f"raw_in{r}") for r in range(RAW)]
        hi_ready = sem("hi_ready")
        lo_ready = sem("lo_ready")
        turn_full = [sem(f"turn_full{b}") for b in range(TURNS)]
        turn_read = [sem(f"turn_read{b}") for b in range(TURNS)]
        turn_half = sem("turn_half")
        pair_prod = sem("pair_prod")
        pair_hi = sem("pair_hi")
        pair_lo = sem("pair_lo")
        pair_used = sem("pair_used")
        acc_half = sem("acc_half")
        first_tap = sem("first_tap")
        second_tap = sem("second_tap")
        gate_ready = sem("gate_ready")
        var_ready = sem("var_ready")
        std_ready = sem("std_ready")
        x_ready = sem("x_ready")
        ident_ready = sem("ident_ready")
        blocks_zero = sem("blocks_zero")
        roped = sem("roped")
        wi_ready = sem("wi_ready")
        relu_ready = sem("relu_ready")
        relu_used = sem("relu_used")
        mask_ready = sem("mask_ready")
        max_ready = sem("max_ready")
        exp_done = sem("exp_done")
        probs_ready = sem("probs_ready")
        sums_inv = sem("sums_inv")
        scaled_ready = sem("scaled_ready")
        dve_step = sem("dve_step")
        out_done = sem("out_done")

        def at(base, it, per):
            return base if it is None else it * per + base

        release = {}
        pair_of_out = {}
        lo_event = {}
        proj_turn = {}
        for si, (kind, stages) in enumerate(SUBS):
            outs = [st for st in stages if st[0] in ("values", "ryT")]
            first_pair = outs[0][4] if outs else 0
            for name, g, n, k, p in stages:
                if name in ("q", "k", "v", "qi", "rv", "rgate"):
                    release[n] = ("turn", k)
                elif name == "misc":
                    release[n] = ("turn", k + 1)
                elif name == "out":
                    release[n] = ("pair", first_pair + g)
                elif name == "ffn":
                    for s in range(STEPS):
                        a, b, c = ffn_slots(n, s)
                        release[a] = ("turn", k + 2 * s)
                        release[b] = ("turn", k + 2 * s + 1)
                        release[c] = ("pair", p + s)
        last_pair = {}
        product_pairs = []
        p_end = 0
        for si, (kind, stages) in enumerate(SUBS):
            for name, g, n, k, p in stages:
                made = {"values": 1, "ryT": 2, "ffn": STEPS}.get(name, 0)
                if name != "values":
                    product_pairs += range(p_end, p_end + made)
                p_end += made
            last_pair[si] = p_end

        def products(p):
            return sum(1 for q in product_pairs if q <= p)

        def wait_full(eng, k, it=None):
            eng.wait_ge(turn_full[k % TURNS], at(k // TURNS + 1, it, 1))

        def wait_read(eng, k, it=None):
            eng.wait_ge(turn_read[k % TURNS], at(k // TURNS + 1, it, 1))

        def wait_slot_used(eng, n, it=None):
            what, i = release[n]
            if what == "turn":
                wait_full(eng, i, it)
            else:
                eng.wait_ge(pair_used, at(i + 1, it, 2))

        nth = {}
        ordinal = {}
        for si, (kind, stages) in enumerate(SUBS):
            for j, (name, g, n, k, p) in enumerate(stages):
                key = "rope" if name in ("q", "k", "qi") else name
                m = 2 if name == "spread" else 1
                key = "rope" if name == "spread" else key
                ordinal[si, j] = nth.get(key, 0)
                nth[key] = nth.get(key, 0) + m

        def dsa_count(si):
            return sum(1 for kind, _ in SUBS[:si + 1] if kind == "dsa")

        def mask_count(si):
            return sum(1 for kind, _ in SUBS[:si + 1] if kind in ("dsa", "moba"))

        def rope_needed(si, j):
            stages = SUBS[si][1]
            name, g = stages[j][:2]
            want = {"index": [("qi", g), ("spread", 0)], "scores": [("q", g), ("k", g), ("spread", 0)],
                    "rscores": [("q", g), ("k", g)]}[name]
            return max(ordinal[si, i] + (2 if st[0] == "spread" else 1)
                       for i, st in enumerate(stages) if (st[0], st[1]) in want)

        def find_turn(si, name, g):
            return next(st[3] for st in SUBS[si][1] if st[0] == name and st[1] == g)

        def v_turn(si, g):
            return find_turn(si, "misc", 0) + 1 if SUBS[si][0] == "dsa" else find_turn(si, "v", g)

        def rv_turn(si, g):
            return find_turn(si, "rv", g)

        def values_turn(si, g):
            return find_turn(si, "values", g)

        def var_count(what, si, g, t):
            n = sum(TT + (TT * RET_HEADS if kind == "ret" else 0) for kind, _ in SUBS[:si])
            if what == "ret":
                return n + TT * g + t + 1
            return n + (TT * RET_HEADS if SUBS[si][0] == "ret" else 0) + t + 1

        def find_pair(si, h):
            return next(st[4] for st in SUBS[si][1] if st[0] == "ryT" and st[1] == h)

        subs = SUBS[:n_subs]
        block = ctx.enter_context(nc.Block())

        @block.sync
        def _(sp):
            for t in range(TT):
                sp.dma_start(x[:, t, :], x_in[t * P:(t + 1) * P, :]).then_inc(x_in_sem, 16)
            for n in range(RAW):
                sp.dma_start(raw[:, n, :], w_slots[n * P:(n + 1) * P, :]).then_inc(raw_in[n], 16)

            def load(n_here, row, r):
                sp.wait_ge(lo_ready, n_here)
                sp.dma_start(raw[:, r, :], w_slots[row, :]).then_inc(raw_in[r], 16)

            rounds = n_slots // RAW - 1
            with sp.Fori(0, rounds) as it:
                for r in range(RAW):
                    load(it * RAW + (r + 1), bass.ds(it * (RAW * P) + (RAW + r) * P, P), r)
            for n in range(RAW * (rounds + 1), n_slots):
                load(n - RAW + 1, bass.ds(n * P, P), n % RAW)
            for t in range(TT):
                sp.wait_ge(x_ready, TT * (n_subs - 1) + t + 1)
                sp.dma_start(out[t * P:(t + 1) * P, :], x[:, t, :]).then_inc(out_done, 16)
            sp.wait_ge(out_done, 16 * TT)

        @block.tensor
        def _(pe):
            def mm(o, a, b, start, stop):
                return pe.matmul(o, a, b, start=start, stop=stop)

            def take_turn(k, it=None):
                if k >= TURNS or it is not None:
                    pe.wait_ge(turn_read[k % TURNS], at(k // TURNS, it, 1))

            def slot_in(n, it=None):
                pe.wait_ge(lo_ready, at(n + 1, it, RING))

            def up_hi(n, k, a, b):
                return w_hi[:, n % RING, 256 * k + a:256 * k + b]

            def up_lo(n, k, a, b):
                return w_lo[:, n % RING, 256 * k + a:256 * k + b]

            def to_features(n, o, a, b):
                for k in range(KD):
                    mm(o, up_hi(n, k, a, b), xT_hi[:, k, :], k == 0, False)
                    mm(o, up_hi(n, k, a, b), xT_lo[:, k, :], False, False)
                    last = mm(o, up_lo(n, k, a, b), xT_hi[:, k, :], False, k == KD - 1)
                return last

            def to_tokens(n, o, t, a, b):
                tok = slice(t * P, (t + 1) * P)
                for k in range(KD):
                    mm(o, xT_hi[:, k, tok], up_hi(n, k, a, b), k == 0, False)
                    mm(o, xT_hi[:, k, tok], up_lo(n, k, a, b), False, False)
                    last = mm(o, xT_lo[:, k, tok], up_hi(n, k, a, b), False, k == KD - 1)
                return last

            def project(n, k, it=None):
                slot_in(n, it)
                take_turn(k, it)
                for j in range(2):
                    last = to_features(n, work[:, k % TURNS, j * SEQ:(j + 1) * SEQ], j * P, (j + 1) * P)
                last.then_inc(turn_full[k % TURNS], 1)

            def accumulate(n, p, first, final, it=None):
                slot_in(n, it)
                for t in range(TT):
                    tok = slice(t * P, (t + 1) * P)
                    for j in range(2):
                        hi, lo = act_hi[:, p % 2, j, tok], act_lo[:, p % 2, j, tok]
                        for half in range(2):
                            c = j * D + half * HALVES
                            wh = w_hi[:, n % RING, c:c + HALVES]
                            wl = w_lo[:, n % RING, c:c + HALVES]
                            o = acc[:, t, half * HALVES:(half + 1) * HALVES]
                            mm(o, hi, wh, first and j == 0, False)
                            mm(o, hi, wl, False, False)
                            last = mm(o, lo, wh, False, final and j == 1)
                    if final and t == 0:
                        last.then_inc(acc_half, 1)
                last.then_inc(pair_used, 1)

            def ffn(n0, k0, p0):
                def step(s, it=None, s0=None):
                    a, b, _ = ffn_slots(n0, s)
                    project(a, k0 + 2 * s, it)
                    project(b, k0 + 2 * s + 1, it)
                    if s:
                        pe.wait_ge(pair_lo, at(products(p0 + s - 1), it, 2))
                        accumulate(b + 1, p0 + s - 1, s == 1 and it is None, False, it)

                step(0)
                step(1)
                with pe.Fori(0, (STEPS - 3) // 2) as it:
                    step(2, it)
                    step(3, it)
                step(STEPS - 1)
                pe.wait_ge(pair_lo, products(p0 + STEPS - 1))
                accumulate(n0 + 3 * STEPS - 1, p0 + STEPS - 1, False, True)

            pe.wait_ge(consts_in, 16)
            pe.wait_ge(ident_ready, 1)
            for si, (kind, stages) in enumerate(subs):
                for j, (name, g, n, k, p) in enumerate(stages):
                    if name == "xT":
                        for t in range(TT):
                            if si:
                                pe.wait_ge(x_ready, TT * (si - 1) + t + 1)
                            else:
                                pe.wait_ge(x_in_sem, 16 * TT)
                            for half in range(2):
                                kk = k + 2 * t + half
                                take_turn(kk)
                                for c in range(4):
                                    f = (4 * half + c) * P
                                    last = pe.transpose(work[:, kk % TURNS, c * P:(c + 1) * P],
                                                        x[:, t, f:f + P], ident)
                                last.then_inc(turn_full[kk % TURNS], 1)
                        for kk in range(k, k + 4):
                            wait_read(pe, kk)
                    elif name == "ffn":
                        ffn(n, k, p)
                    elif name in ("q", "k", "qi", "rgate"):
                        project(n, k)
                    elif name in ("v", "rv"):
                        slot_in(n)
                        take_turn(k)
                        for t in range(TT):
                            last = to_tokens(n, work[:, k % TURNS, 256 * t:256 * t + 256], t, 0, 256)
                        last.then_inc(turn_full[k % TURNS], 1)
                    elif name == "misc":
                        slot_in(n)
                        take_turn(k)
                        to_features(n, work[:, k % TURNS, 0:SEQ], 0, P).then_inc(turn_full[k % TURNS], 1)
                        take_turn(k + 1)
                        for t in range(TT):
                            last = to_tokens(n, work[:, (k + 1) % TURNS, 256 * t:256 * t + 72], t, P, P + 72)
                        last.then_inc(turn_full[(k + 1) % TURNS], 1)
                    elif name == "spread":
                        wait_read(pe, k - 2)
                        pe.wait_ge(table_in, 16 * (si // 2 + 1))
                        for u in range(2):
                            take_turn(k + u)
                            for half in range(2):
                                sel = table[:, 512 + P * (2 * u + half):512 + P * (2 * u + half + 1)]
                                last = mm(work[:, (k + u) % TURNS, half * SEQ:(half + 1) * SEQ], sel, narrow, True, True)
                            last.then_inc(turn_full[(k + u) % TURNS], 1)
                    elif name in ("scores", "index"):
                        pe.wait_ge(roped, rope_needed(si, j))
                        if name == "scores":
                            pe.wait_ge(mask_ready, mask_count(si))
                            qs, ks = qT[g if kind == "dsa" else g % 2], k_diag
                        else:
                            qs, ks = qT[2 + g], ki_diag
                        for part in range(3):
                            b = (k + part) % TURNS
                            take_turn(k + part)
                            keys = P if part == 0 else SEQ
                            heads = range(4) if part == 0 else range(2 * part - 2, 2 * part)
                            q0 = 0 if part == 0 else P
                            o = work[:, b, :].rearrange("p (h k) -> p h k", k=keys)
                            if name == "scores":
                                m = mask_r[:, 0:P] if part == 0 else mask_r[:, P:3 * P]
                                mm(o, ident_r[:, :], m.unsqueeze(1).to_broadcast([P, len(heads), keys]), True, False)
                            for half in range(2):
                                last = mm(o, qs[:, half, q0:q0 + P], ks[:, half, heads.start:heads.stop, 0:keys],
                                          name == "index" and half == 0, half == 1)
                            last.then_inc(turn_full[b], 1)
                    elif name == "probsT":
                        for part in range(3):
                            b = (k + part) % TURNS
                            take_turn(k + part)
                            pe.wait_ge(probs_ready, 3 * ordinal[si, j] + part + 1)
                            for c in range(4):
                                last = pe.transpose(work[:, b, c * P:(c + 1) * P],
                                                    probs[:, 512 * part + c * P:512 * part + (c + 1) * P], ident)
                            last.then_inc(turn_full[b], 1)
                    elif name == "values":
                        for part in range(3):
                            wait_read(pe, k - 3 + part)
                        wait_read(pe, v_turn(si, g))
                        take_turn(k)
                        for h in range(4):
                            vh = (lambda t: v[0][:, t, 0:HEAD_DIM]) if kind == "dsa" else \
                                (lambda t: v[g % 2][:, t, h * HEAD_DIM:(h + 1) * HEAD_DIM])
                            rows = slice(64 * (h % 2), 64 * (h % 2) + 64)
                            o = work[rows, k % TURNS, :]
                            c0 = (h // 2) * SEQ
                            mm(o[:, c0:c0 + P], vh(0), probsT[:, h * P:(h + 1) * P], True, True)
                            late = 512 + h * SEQ
                            mm(o[:, c0 + P:c0 + SEQ], vh(0), probsT[:, late:late + P], True, False)
                            last = mm(o[:, c0 + P:c0 + SEQ], vh(1), probsT[:, late + P:late + SEQ], False, True)
                        last.then_inc(turn_full[k % TURNS], 1)
                    elif name == "out":
                        _, pp = release[n]
                        first = g == 0
                        final = j == len(stages) - 1
                        if kind == "ret":
                            pe.wait_ge(pair_lo, products(pp))
                        else:
                            wait_read(pe, values_turn(si, g))
                        accumulate(n, pp, first, final)
                    elif name == "rscores":
                        pe.wait_ge(roped, rope_needed(si, j))
                        take_turn(k)
                        b = k % TURNS
                        for d in range(2):
                            mm(work[:, b, 0:SEQ], kT[g % 2][:, d, 0:P], qT[g % 2][:, d, :], d == 0, d == 1)
                        for d in range(2):
                            last = mm(work[:, b, SEQ:SEQ + P], kT[g % 2][:, d, P:SEQ], qT[g % 2][:, d, P:SEQ],
                                      d == 0, d == 1)
                        last.then_inc(turn_full[b], 1)
                    elif name == "rvalues":
                        wait_read(pe, find_turn(si, "rscores", g))
                        for u in range(2):
                            wait_read(pe, rv_turn(si, 2 * g + u))
                        take_turn(k)
                        mm(work[:, k % TURNS, :], decayed[:, 0:P], ret_v[:, 0, :], True, True)\
                            .then_inc(turn_full[k % TURNS], 1)
                        take_turn(k + 1)
                        o = work[:, (k + 1) % TURNS, :]
                        mm(o, decayed[:, P:2 * P], ret_v[:, 0, :], True, False)
                        mm(o, decayed[:, 2 * P:3 * P], ret_v[:, 1, :], False, True)\
                            .then_inc(turn_full[(k + 1) % TURNS], 1)
                    elif name == "ryT":
                        for t in range(TT):
                            wait_read(pe, find_turn(si, "rvalues", g) + t)
                        for u in range(2):
                            b = (k + u) % TURNS
                            take_turn(k + u)
                            for c in range(2):
                                for t in range(TT):
                                    f = (2 * u + c) * P
                                    last = pe.transpose(work[:, b, c * SEQ + t * P:c * SEQ + (t + 1) * P],
                                                        normed[:, t, f:f + P], ident)
                            last.then_inc(turn_full[b], 1)

        @block.scalar
        def _(act):
            fed = [0]

            def split_hi(n, it=None):
                act.wait_ge(raw_in[n % RAW], at(16 * (n // RAW + 1), it, 16 * (RING // RAW)))
                if n >= RING:
                    wait_slot_used(act, n - RING, it)
                act.activation(w_hi[:, n % RING, :], raw[:, n % RAW, :], ACT.Copy).then_inc(hi_ready, 1)

            def feed(upto):
                while fed[0] < min(upto + 1, n_slots):
                    split_hi(fed[0])
                    fed[0] += 1

            def ffn(n0, k0, p0, layer):
                def step(s, it=None):
                    a = ffn_slots(n0, s)[0]

                    def feed_one(i):
                        if it is not None:
                            split_hi(a + 3 + i, it)
                        else:
                            feed(a + 3 + i if s else a + 2 + i)

                    b = (p0 + s) % 2
                    for u in range(2):
                        k = k0 + 2 * s + u
                        if u == 0 and s >= 2:
                            act.wait_ge(pair_prod, at(products(p0 + s - 2), it, 2))
                        wait_full(act, k, it)
                        for j in range(2):
                            last = conv_col(b, u, j, k, s, it)
                        last.then_inc(first_tap, 1)
                        feed_one(u)
                    wait_read(act, k0 + 2 * s, it)
                    act.activation(gate[b][:, :, :], taps[b][0][:, :, :], ACT.Silu).then_inc(gate_ready, 1)
                    feed_one(2)
                    act.wait_ge(pair_prod, at(products(p0 + s), it, 2))
                    act.wait_ge(pair_used, at(p0 + s - 1, it, 2))
                    act.activation(act_hi[:, b, :, :], prod[b][:, :, :], ACT.Copy).then_inc(pair_hi, 1)

                def conv_col(b, u, j, k, s, it):
                    c = 2 * s + j + u * (D_FF // P)
                    if it is None:
                        w2, bias = conv[:, c, 2:3], conv[:, c, 3:4]
                    else:
                        w2 = conv[:, bass.ds(it * 4 + c, 1), 2:3].rearrange("p a b -> p (a b)")
                        bias = conv[:, bass.ds(it * 4 + c, 1), 3:4].rearrange("p a b -> p (a b)")
                    return act.activation(taps[b][u][:, j, :], work[:, k % TURNS, j * SEQ:(j + 1) * SEQ],
                                          ACT.Identity, bias=bias, scale=w2)

                act.wait_ge(conv_in, 16 * (layer + 1))
                step(0)
                step(1)
                with act.Fori(0, (STEPS - 3) // 2) as it:
                    step(2, it)
                    step(3, it)
                fed[0] = ffn_slots(n0, STEPS - 1)[0] + 3
                step(STEPS - 1)

            act.wait_ge(consts_in, 16)
            act.activation(ident_r[:, :], ident, ACT.Copy).then_inc(ident_ready, 1)
            feed(3)
            for si, (kind, stages) in enumerate(subs):
                for j, (name, g, n, k, p) in enumerate(stages):
                    if name in ("q", "k", "qi", "v", "rv", "rgate", "misc", "out"):
                        feed(n + 4)
                    if name == "xT":
                        for kk in range(k, k + 4):
                            t, half = divmod(kk - k, 2)
                            wait_full(act, kk)
                            act.activation(xT_hi[:, 4 * half:4 * half + 4, t * P:(t + 1) * P],
                                           work[:, kk % TURNS, :].rearrange("p (c t) -> p c t", c=4), ACT.Copy)\
                                .then_inc(turn_half, 1)
                    elif name == "ffn":
                        ffn(n, k, p, si // 2)
                    elif name == "misc":
                        wait_full(act, k)
                        act.activation(narrow, work[:, k % TURNS, 0:SEQ], ACT.Copy).then_inc(turn_read[k % TURNS], 1)
                        wait_full(act, k + 1)
                        o = work[:, (k + 1) % TURNS, :].rearrange("p (t c) -> p t c", t=2)
                        act.activation(stat[:, 64:64 + 16].rearrange("p (t h) -> p t h", t=2), o[:, :, 64:72], ACT.Copy,
                                       scale=IDX_SCALE).then_inc(wi_ready, 1)
                        act.activation(v[0][:, :, 0:HEAD_DIM], o[:, :, 0:HEAD_DIM], ACT.Copy)\
                            .then_inc(turn_read[(k + 1) % TURNS], 1)
                    elif name in ("v", "rv"):
                        wait_full(act, k)
                        o = work[:, k % TURNS, :].rearrange("p (t c) -> p t c", t=2)
                        dst = v[g % 2][:, :, :] if name == "v" else ret_v[:, :, 256 * (g % 2):256 * (g % 2) + 256]
                        act.activation(dst, o, ACT.Copy).then_inc(turn_read[k % TURNS], 1)
                    elif name == "index":
                        for part in range(3):
                            i = 3 * ordinal[si, j] + part
                            wait_full(act, k + part)
                            if i >= 3:
                                act.wait_ge(relu_used, i - 2)
                            act.activation(relu[part], work[:, (k + part) % TURNS, :], ACT.Relu)\
                                .then_inc(turn_read[(k + part) % TURNS], 1)
                    elif name == "scores":
                        o0 = ordinal[si, j]
                        if g:
                            wait_full(act, find_turn(si, "probsT", g - 1) + 2)
                        for part in range(3):
                            i = 3 * o0 + part
                            act.wait_ge(max_ready, i + 1)
                            keys = P if part == 0 else SEQ
                            heads = 4 if part == 0 else 2
                            c0 = 0 if part == 0 else 2 + 2 * part
                            for h in range(heads):
                                c = c0 + h
                                ins = act.activation(probs[:, 512 * part + h * keys:512 * part + (h + 1) * keys],
                                                     work[:, (k + part) % TURNS, h * keys:(h + 1) * keys], ACT.Exp,
                                                     bias=stat[:, 16 + c:17 + c], scale=SCALE,
                                                     accum_out=stat[:, 24 + c:25 + c])
                            ins.then_inc(turn_read[(k + part) % TURNS], 1)
                    elif name == "probsT":
                        if g:
                            wait_full(act, find_turn(si, "values", g - 1))
                        for part in (0, 2):
                            wait_full(act, k + part)
                            act.activation(probsT[:, 512 * part:512 * part + 512], work[:, (k + part) % TURNS, :], ACT.Copy)\
                                .then_inc(turn_read[(k + part) % TURNS], 1)
                    elif name == "values":
                        wait_full(act, k)
                        if p >= 2:
                            act.wait_ge(pair_used, p - 1)
                        act.activation(act_hi[:, p % 2, :, :], work[:, k % TURNS, :].rearrange("p (c t) -> p c t", c=2),
                                       ACT.Copy).then_inc(pair_hi, 1)
                    elif name == "rgate":
                        if g >= 2 and g % 2 == 0:
                            act.wait_ge(pair_prod, products(find_pair(si, g // 2 - 1) + 1))
                        wait_full(act, k)
                        act.activation(ret_gate[:, 2 * (g % 2):2 * (g % 2) + 2, :],
                                       work[:, k % TURNS, :].rearrange("p (c t) -> p c t", c=2), ACT.Silu)\
                            .then_inc(turn_read[k % TURNS], 1)
                    elif name == "rvalues":
                        for t in range(TT):
                            c = 2 * t
                            i = var_count("ret", si, g, t)
                            act.wait_ge(var_ready, i)
                            act.activation(stat[:, 80 + t:81 + t], stat[:, 40 + c + 1:42 + c], ACT.Sqrt,
                                           bias=stat[:, 95:96]).then_inc(std_ready, 1)
                    elif name == "ryT":
                        act.wait_ge(gn_in, 16)
                        for u in range(2):
                            wait_full(act, k + u)
                            pp = p + u
                            act.wait_ge(pair_prod, products(pp - 2))
                            for c in range(2):
                                col = 4 * g + 2 * u + c
                                ins = act.activation(scaled[u][:, c, :], work[:, (k + u) % TURNS, c * SEQ:(c + 1) * SEQ],
                                                     ACT.Identity, bias=gn[:, col, 1:2], scale=gn[:, col, 0:1])
                            ins.then_inc(turn_read[(k + u) % TURNS], 1)
                        for u in range(2):
                            pp = p + u
                            act.wait_ge(pair_prod, products(pp))
                            act.wait_ge(pair_used, pp - 1)
                            act.activation(act_hi[:, pp % 2, :, :], ret_prod[u][:, :, :], ACT.Copy).then_inc(pair_hi, 1)
                for t in range(TT):
                    act.wait_ge(var_ready, var_count("ln", si, 0, t))
                    act.activation(stat[:, 4 + t:5 + t], stat[:, 2 * t + 1:2 * t + 2], ACT.Sqrt,
                                   bias=stat[:, 94:95]).then_inc(std_ready, 1)

        @block.vector
        def _(dve):
            fed = [0]
            steps = [0]

            def settle(ins):
                steps[0] += 1
                ins.then_inc(dve_step, 1)
                dve.wait_ge(dve_step, steps[0])

            def split_lo(n, it=None):
                dve.wait_ge(hi_ready, at(n + 1, it, RING))
                dve.tensor_tensor(w_lo[:, n % RING, :], raw[:, n % RAW, :], w_hi[:, n % RING, :], ALU.subtract)\
                    .then_inc(lo_ready, 1)

            def feed(upto):
                while fed[0] < min(upto + 1, n_slots):
                    split_lo(fed[0])
                    fed[0] += 1

            def ffn(n0, k0, p0, layer):
                def col(s, u, j, tap, it):
                    c = 2 * s + j + u * (D_FF // P)
                    if it is None:
                        return conv[:, c, tap:tap + 1]
                    return conv[:, bass.ds(it * 4 + c, 1), tap:tap + 1].rearrange("p a b -> p (a b)")

                def step(s, it=None):
                    a = ffn_slots(n0, s)[0]
                    b = (p0 + s) % 2

                    def feed_one(i):
                        if it is not None:
                            split_lo(a + 3 + i, it)
                        else:
                            feed(a + 3 + i if s else a + 2 + i)

                    for u in range(2):
                        k = k0 + 2 * s + u
                        i = 2 * (STEPS * layer + s) + u
                        dve.wait_ge(first_tap, at(i + 1, it, 4))
                        for j in range(2):
                            o, h = taps[b][u][:, j, :], work[:, k % TURNS, j * SEQ:(j + 1) * SEQ]
                            ins = dve.scalar_tensor_tensor(out=o[:, 1:SEQ], in0=h[:, 0:SEQ - 1], scalar=col(s, u, j, 1, it),
                                                           in1=o[:, 1:SEQ], op0=ALU.mult, op1=ALU.add)
                        ins.then_inc(second_tap, 1)
                        dve.wait_ge(second_tap, at(i + 1, it, 4))
                        for j in range(2):
                            o, h = taps[b][u][:, j, :], work[:, k % TURNS, j * SEQ:(j + 1) * SEQ]
                            ins = dve.scalar_tensor_tensor(out=o[:, 2:SEQ], in0=h[:, 0:SEQ - 2], scalar=col(s, u, j, 0, it),
                                                           in1=o[:, 2:SEQ], op0=ALU.mult, op1=ALU.add)
                        ins.then_inc(turn_read[k % TURNS], 1)
                        feed_one(u)
                    feed_one(2)
                    dve.wait_ge(gate_ready, at(STEPS * layer + s + 1, it, 2))
                    wait_read(dve, k0 + 2 * s + 1, it)
                    dve.wait_ge(pair_lo, at(products(p0 + s - 2), it, 2)) if products(p0 + s - 2) else None
                    dve.tensor_tensor(prod[b][:, :, :], gate[b][:, :, :], taps[b][1][:, :, :], ALU.mult)\
                        .then_inc(pair_prod, 1)

                step(0)
                step(1)
                with dve.Fori(0, (STEPS - 3) // 2) as it:
                    step(2, it)
                    step(3, it)
                fed[0] = ffn_slots(n0, STEPS - 1)[0] + 3
                step(STEPS - 1)

            def norm(si):
                last = si == n_subs - 1
                dve.wait_ge(ln_in, 16 * (si + 1))
                for t in range(TT):
                    if t == 0:
                        dve.wait_ge(acc_half, si + 1)
                    else:
                        dve.wait_ge(pair_used, last_pair[si])
                    settle(dve.scalar_tensor_tensor(out=x[:, t, :], in0=x[:, t, :], scalar=float(ALPHA), in1=acc[:, t, :],
                                                    op0=ALU.mult, op1=ALU.add))
                    for h in range(2):
                        ins = dve.bn_stats(stat[:, 48 + 6 * h:54 + 6 * h], x[:, t, h * 512:(h + 1) * 512])
                    settle(ins)
                    dve.bn_aggr(stat[:, 2 * t:2 * t + 2], stat[:, 48:60]).then_inc(var_ready, 1)
                    dve.wait_ge(var_ready, var_count("ln", si, 0, t))
                    settle(dve.scalar_tensor_tensor(out=x[:, t, :], in0=x[:, t, :], scalar=stat[:, 2 * t:2 * t + 1],
                                                    in1=ln[:, 0, :], op0=ALU.subtract, op1=ALU.mult))
                    dve.wait_ge(std_ready, var_count("ln", si, 0, t))
                    settle(dve.reciprocal(stat[:, 6 + t:7 + t], stat[:, 4 + t:5 + t]))
                    dve.scalar_tensor_tensor(out=x[:, t, :], in0=x[:, t, :], scalar=stat[:, 6 + t:7 + t],
                                             in1=ln[:, 1, :], op0=ALU.mult, op1=ALU.add).then_inc(x_ready, 1)

            def rotate(k, r, table_n):
                wait_full(dve, k)
                dve.wait_ge(table_in, 16 * table_n)
                if r:
                    dve.wait_ge(roped, r)
                src = work[:, k % TURNS, :].rearrange("p (c t) -> p c t", c=2)
                dve.tensor_tensor(by_cos[:, :, :], src, cos.unsqueeze(1).to_broadcast([P, 2, SEQ]), ALU.mult)
                dve.tensor_tensor(by_sin[:, :, :], src, sin.unsqueeze(1).to_broadcast([P, 2, SEQ]), ALU.mult)\
                    .then_inc(turn_read[k % TURNS], 1)

            def topk(first, keys, rounds):
                for r in rounds:
                    src = index if r == 0 else left
                    settle(dve.max(stat[:, 84:92], src[:, first:first + keys]))
                    settle(dve.match_replace(left[:, first:first + keys], stat[:, 84:92], src[:, first:first + keys], TAKEN))

            dve.memset(stat[:, 94:95], LN_EPS)
            settle(dve.memset(stat[:, 95:96], GN_EPS))
            dve.wait_ge(consts_in, 16)
            feed(3)
            for si, (kind, stages) in enumerate(subs):
                for j, (name, g, n, k, p) in enumerate(stages):
                    if name in ("q", "k", "qi", "v", "rv", "rgate", "misc", "out"):
                        feed(n + 4)
                    if name == "xT":
                        for kk in range(k, k + 4):
                            t, half = divmod(kk - k, 2)
                            dve.wait_ge(turn_half, 4 * si + kk - k + 1)
                            dst = (slice(None), slice(4 * half, 4 * half + 4), slice(t * P, (t + 1) * P))
                            dve.tensor_tensor(xT_lo[dst], work[:, kk % TURNS, :].rearrange("p (c t) -> p c t", c=4),
                                              xT_hi[dst], ALU.subtract).then_inc(turn_read[kk % TURNS], 1)
                    elif name == "ffn":
                        ffn(n, k, p, si // 2)
                    elif name == "spread":
                        for u in range(2):
                            rotate(k + u, ordinal[si, j] + u, si // 2 + 1)
                    elif name in ("q", "k", "qi"):
                        rotate(k, ordinal[si, j], si // 2 + 1)
                    elif name == "index":
                        if g == 0:
                            dve.wait_ge(wi_ready, dsa_count(si))
                        for part in range(3):
                            i = 3 * ordinal[si, j] + part
                            wait_read(dve, k + part)
                            heads = range(4) if part == 0 else range(2 * part - 2, 2 * part)
                            t = 0 if part == 0 else 1
                            dst = index[:, 0:P] if part == 0 else index[:, P:3 * P]
                            base = causal[:, 0:P] if part == 0 else causal[:, P:3 * P]
                            keys = P if part == 0 else SEQ
                            for m, h in enumerate(heads):
                                start = g == 0 and h == 0
                                ins = dve.scalar_tensor_tensor(
                                    out=dst, in0=relu[part][:, m * keys:(m + 1) * keys],
                                    scalar=stat[:, 64 + 8 * t + 4 * g + h:65 + 8 * t + 4 * g + h],
                                    in1=base if start else dst, op0=ALU.mult, op1=ALU.add)
                                if m < len(heads) - 1:
                                    settle(ins)
                            ins.then_inc(relu_used, 1)
                            dve.wait_ge(relu_used, i + 1)
                    elif name == "topk":
                        half = TOPK // 16
                        if g == 0:
                            topk(0, P, range(TOPK // 8))
                        elif g == 1:
                            topk(P, SEQ, range(half))
                        elif g == 2:
                            topk(P, SEQ, range(half, TOPK // 8))
                            settle(dve.tensor_scalar(index, left, TAKEN / 2, NEG, ALU.is_ge, ALU.mult))
                            dve.tensor_tensor(mask_r[:, :], index, causal, ALU.add).then_inc(mask_ready, 1)
                    elif name == "mask":
                        dve.tensor_copy(mask_r[:, :], causal).then_inc(mask_ready, 1)
                    elif name == "scores":
                        for part in range(3):
                            wait_full(dve, k + part)
                            keys = P if part == 0 else SEQ
                            heads = 4 if part == 0 else 2
                            c0 = 0 if part == 0 else 2 + 2 * part
                            settle(dve.tensor_reduce(stat[:, 8 + c0:8 + c0 + heads],
                                                     work[:, (k + part) % TURNS, :].rearrange("p (h k) -> p h k", k=keys),
                                                     AX_X, ALU.max))
                            dve.tensor_scalar(stat[:, 16 + c0:16 + c0 + heads], stat[:, 8 + c0:8 + c0 + heads],
                                              -SCALE, None, ALU.mult).then_inc(max_ready, 1)
                        for part in range(3):
                            wait_read(dve, k + part)
                            heads = 4 if part == 0 else 2
                            c0 = 0 if part == 0 else 2 + 2 * part
                            dve.reciprocal(stat[:, 32 + c0:32 + c0 + heads], stat[:, 24 + c0:24 + c0 + heads])\
                                .then_inc(sums_inv, 1)
                    elif name == "probsT":
                        wait_full(dve, k + 1)
                        if g:
                            wait_full(dve, find_turn(si, "values", g - 1))
                        dve.tensor_copy(probsT[:, 512:1024], work[:, (k + 1) % TURNS, :])\
                            .then_inc(turn_read[(k + 1) % TURNS], 1)
                    elif name == "values":
                        dve.wait_ge(pair_hi, p + 1)
                        dve.tensor_tensor(act_lo[:, p % 2, :, :], work[:, k % TURNS, :].rearrange("p (c t) -> p c t", c=2),
                                          act_hi[:, p % 2, :, :], ALU.subtract).then_inc(turn_read[k % TURNS], 1)
                    elif name == "rscores":
                        wait_full(dve, k)
                        o = work[:, k % TURNS, :]
                        d0 = 512 + 256 * g
                        dve.tensor_tensor(decayed[:, 0:SEQ], o[:, 0:SEQ], table[:, d0:d0 + SEQ], ALU.mult)
                        dve.tensor_tensor(decayed[:, SEQ:SEQ + P], o[:, SEQ:SEQ + P], table[:, d0:d0 + P], ALU.mult)\
                            .then_inc(turn_read[k % TURNS], 1)
                    elif name == "rvalues":
                        for t in range(TT):
                            o = work[:, (k + t) % TURNS, :]
                            wait_full(dve, k + t)
                            settle(dve.bn_stats(stat[:, 48 + 6 * t:54 + 6 * t], o))
                            dve.bn_aggr(stat[:, 40 + 2 * t:42 + 2 * t], stat[:, 48 + 6 * t:54 + 6 * t]).then_inc(var_ready, 1)
                        if g:
                            wait_full(dve, find_turn(si, "ryT", g - 1) + 1)
                        for t in range(TT):
                            o = work[:, (k + t) % TURNS, :]
                            dve.wait_ge(std_ready, var_count("ret", si, g, t))
                            settle(dve.reciprocal(stat[:, 82 + t:83 + t], stat[:, 80 + t:81 + t]))
                            dve.tensor_scalar(normed[:, t, :], o, stat[:, 40 + 2 * t:41 + 2 * t], stat[:, 82 + t:83 + t],
                                              ALU.subtract, ALU.mult).then_inc(turn_read[(k + t) % TURNS], 1)
                    elif name == "ryT":
                        for u in range(2):
                            pp = p + u
                            wait_read(dve, k + u)
                            dve.wait_ge(pair_lo, products(pp - 2))
                            dve.tensor_tensor(ret_prod[u][:, :, :], scaled[u][:, :, :], ret_gate[:, 2 * u:2 * u + 2, :],
                                              ALU.mult).then_inc(pair_prod, 1)
                norm(si)

        @block.gpsimd
        def _(pool):
            def load_ln(si):
                pool.dma_start(ln[:, :, :].rearrange("p a d -> p (a d)"), ln_rows[si, :].partition_broadcast(P))\
                    .then_inc(ln_in, 16)

            def load_table(i):
                pool.dma_start(table[:, :], tables[P * (MIXERS[i] == "ret"):P * (MIXERS[i] == "ret") + P, :])\
                    .then_inc(table_in, 16)

            def load_conv(i):
                pool.dma_start(conv[:, :, :].rearrange("p a b -> p (a b)"), conv_cols[P * i:P * (i + 1), :])\
                    .then_inc(conv_in, 16)

            pool.dma_start(const[:, :], consts).then_inc(consts_in, 16)
            load_table(0)
            load_ln(0)
            load_conv(0)
            pool.dma_start(gn[:, :, :].rearrange("p a b -> p (a b)"), gn_cols).then_inc(gn_in, 16)

            zeroed = [0]

            def rest(p, src, it=None):
                pool.wait_ge(pair_hi, at(p + 1, it, 2))
                pool.tensor_tensor(act_lo[:, p % 2, :, :], src[:, :, :], act_hi[:, p % 2, :, :], ALU.subtract)\
                    .then_inc(pair_lo, 1)

            for si, (kind, stages) in enumerate(subs):
                if kind in ("dsa", "moba"):
                    zeroed[0] += 1
                    if kind == "dsa":
                        pool.memset(ki_diag[:, :, :, :], 0.0)
                    pool.memset(k_diag[:, :, :, :], 0.0).then_inc(blocks_zero, 1)
                    pool.wait_ge(blocks_zero, zeroed[0])
                for j, (name, g, n, k, p) in enumerate(stages):
                    if name in ("q", "k", "qi", "spread"):
                        for u in range(2 if name == "spread" else 1):
                            r = ordinal[si, j] + u
                            wait_read(pool, k + u)
                            blocks = {("dsa", "spread"): (k_diag, ki_diag)[u], ("moba", "k"): k_diag}.get((kind, name))
                            if blocks is None:
                                dst = kT[g % 2] if name == "k" else qT[2 + g] if name == "qi" else \
                                    qT[g if kind == "dsa" else g % 2]
                                pool.tensor_tensor(dst[:, 0, :], by_cos[:, 0, :], by_sin[:, 1, :], ALU.subtract)
                                pool.tensor_tensor(dst[:, 1, :], by_cos[:, 1, :], by_sin[:, 0, :], ALU.add)\
                                    .then_inc(roped, 1)
                                continue
                            for h in range(4):
                                rows = slice(32 * h, 32 * h + 32)
                                pool.tensor_tensor(blocks[rows, 0, h, :], by_cos[rows, 0, :], by_sin[rows, 1, :],
                                                   ALU.subtract)
                                ins = pool.tensor_tensor(blocks[rows, 1, h, :], by_cos[rows, 1, :], by_sin[rows, 0, :],
                                                         ALU.add)
                            ins.then_inc(roped, 1)
                    elif name == "scores":
                        for part in range(3):
                            i = 3 * ordinal[si, j] + part
                            keys = P if part == 0 else SEQ
                            heads = 4 if part == 0 else 2
                            c0 = 0 if part == 0 else 2 + 2 * part
                            pool.wait_ge(sums_inv, i + 1)
                            pr = probs[:, 512 * part:512 * part + 512].rearrange("p (h k) -> p h k", k=keys)
                            pool.tensor_tensor(pr, pr, stat[:, 32 + c0:32 + c0 + heads].unsqueeze(2)
                                               .to_broadcast([P, heads, keys]), ALU.mult).then_inc(probs_ready, 1)
                    elif name == "ryT":
                        for u in range(2):
                            rest(p + u, ret_prod[u])
                    elif name == "ffn":
                        rest(p, prod[p % 2])
                        rest(p + 1, prod[(p + 1) % 2])
                        with pool.Fori(0, (STEPS - 3) // 2) as it:
                            rest(p + 2, prod[p % 2], it)
                            rest(p + 3, prod[(p + 1) % 2], it)
                        rest(p + STEPS - 1, prod[(p + STEPS - 1) % 2])
                if si + 1 < n_subs:
                    pool.wait_ge(x_ready, TT * (si + 1))
                    load_ln(si + 1)
                    if si % 2:
                        load_conv(si // 2 + 1)
                    elif si // 2 + 1 < DEPTH:
                        load_table(si // 2 + 1)


def kernel(**inputs):
    import concourse.bacc as bacc
    from concourse.bass_utils import run_bass_kernel_spmd as run

    w = {k: np.asarray(a) for k, a in inputs.items()}
    tables, consts = lay_tables()
    conv_cols = np.concatenate([np.concatenate([w[f"l{i}_conv_w"], w[f"l{i}_conv_b"][None]]).reshape(4, 44, P)
                                .transpose(2, 1, 0).reshape(P, 176) for i in range(DEPTH)])
    ln_rows = np.stack([np.concatenate([w[f"l{i}_ln{j}_g"], w[f"l{i}_ln{j}_b"]]) for i in range(DEPTH) for j in (1, 2)])
    gn_cols = np.stack([w["l2_gn_g"], w["l2_gn_b"]]).reshape(2, 16, P).transpose(2, 1, 0).reshape(P, 32)
    arrays = {
        "x_rows": w["x"].reshape(SEQ, D),
        "w_slots": lay_slots(w).reshape(N_SLOTS * P, SLOT),
        "ln_rows": ln_rows,
        "conv_cols": conv_cols,
        "gn_cols": gn_cols,
        "tables": tables.reshape(2 * P, TABLE),
        "consts": consts,
    }
    arrays = {k: np.ascontiguousarray(a) for k, a in arrays.items()}
    nc = bacc.Bacc("TRN2", target_bir_lowering=False, num_devices=1)
    args = [nc.dram_tensor(k, a.shape, F32, kind="ExternalInput").ap() for k, a in arrays.items()]
    out = nc.dram_tensor("y", (SEQ, D), F32, kind="ExternalOutput").ap()
    build(nc, *args, out, N_SUBS)
    return run(nc, [arrays], core_ids=[0]).results[0]["y"].reshape(1, SEQ, D)


N_SUBS = 2 * DEPTH
```

```python
from contextlib import ExitStack

import numpy as np

import concourse.bass as bass
from concourse import mybir

F32 = mybir.dt.float32
F32R = mybir.dt.float32r
ALU = mybir.AluOpType
ACT = mybir.ActivationFunctionType
AX_X = mybir.AxisListType.X

P = 128
SEQ = 256
TT = SEQ // P
D = 1024
KD = D // P
DEPTH = 4
ALPHA = (2 * DEPTH) ** 0.25
LN_EPS = 1e-5
GN_EPS = 1e-6
NEG = -1e30
TAKEN = -3e38
D_FF = 2816
STEPS = D_FF // 256
HEAD_DIM = 64
SCALE = HEAD_DIM ** -0.5
GROUPS = 4
TOPK = min(256, SEQ // 4)
IDX_HEADS = 8
IDX_SCALE = IDX_HEADS ** -0.5 * 64 ** -0.5
RET_HEADS = 4
SLOT = 2048
HALVES = 512
RING = 6
RAW = 3
TURNS = 4
MIXERS = ("dsa", "moba", "ret", "dsa")
TABLE = 1536


def plan_sublayers():
    subs = []
    slot = turn = pair = 0

    def stage(out, name, g=0, slots=0, turns=0, pairs=0):
        nonlocal slot, turn, pair
        out.append((name, g, slot, turn, pair))
        slot += slots
        turn += turns
        pair += pairs

    for kind in MIXERS:
        s = []
        stage(s, "xT", 0, 0, 4 if subs else 0)
        if kind == "dsa":
            stage(s, "misc", 0, 1, 2)
            stage(s, "spread", 0, 0, 2)
            stage(s, "qi", 0, 1, 1)
            stage(s, "qi", 1, 1, 1)
            stage(s, "index", 0, 0, 3)
            stage(s, "index", 1, 0, 3)
            for g in range(GROUPS):
                stage(s, "q", g, 1, 1)
                stage(s, "topk", g)
            for g in range(GROUPS):
                stage(s, "scores", g, 0, 3)
                if g:
                    stage(s, "out", g - 1, 1)
                stage(s, "probsT", g, 0, 3)
                stage(s, "values", g, 0, 1, 1)
            stage(s, "out", GROUPS - 1, 1)
        elif kind == "moba":
            stage(s, "mask")
            for n in "vqk":
                stage(s, n, 0, 1, 1)
            s.append(s.pop(-3))
            for g in range(GROUPS):
                stage(s, "scores", g, 0, 3)
                if g:
                    stage(s, "out", g - 1, 1)
                if g + 1 < GROUPS:
                    for n in "qkv":
                        stage(s, n, g + 1, 1, 1)
                stage(s, "probsT", g, 0, 3)
                stage(s, "values", g, 0, 1, 1)
            stage(s, "out", GROUPS - 1, 1)
        else:
            stage(s, "rv", 0, 1, 1)
            stage(s, "rv", 1, 1, 1)
            stage(s, "q", 0, 1, 1)
            stage(s, "k", 0, 1, 1)
            s[-4:] = s[-2:] + s[-4:-2]
            for h in range(RET_HEADS):
                if h:
                    stage(s, "rv", 2 * h, 1, 1)
                    stage(s, "rv", 2 * h + 1, 1, 1)
                stage(s, "rscores", h, 0, 1)
                if h:
                    stage(s, "out", 2 * h - 2, 1)
                    stage(s, "out", 2 * h - 1, 1)
                stage(s, "rgate", 2 * h, 1, 1)
                stage(s, "rgate", 2 * h + 1, 1, 1)
                stage(s, "rvalues", h, 0, 2)
                if h + 1 < RET_HEADS:
                    stage(s, "q", h + 1, 1, 1)
                    stage(s, "k", h + 1, 1, 1)
                stage(s, "ryT", h, 0, 2, 2)
            stage(s, "out", 2 * RET_HEADS - 2, 1)
            stage(s, "out", 2 * RET_HEADS - 1, 1)
        subs.append((kind, s))
        f = []
        stage(f, "xT", 0, 0, 4)
        stage(f, "ffn", 0, 3 * STEPS, 2 * STEPS, STEPS)
        subs.append(("ffn", f))
    return subs, slot, turn, pair


SUBS, N_SLOTS, N_TURNS, N_PAIRS = plan_sublayers()


def ffn_slots(first, s):
    up = first if s == 0 else first + 3 * s - 1
    return up, up + 1, first + 3 * s + (4 if s + 1 < STEPS else 2)


def lay_slots(w):
    out = np.zeros((N_SLOTS, P, SLOT), np.float32)

    def up(n, m):
        out[n].reshape(P, KD, 256)[:, :, :m.shape[1]] = m.reshape(KD, P, -1).transpose(1, 0, 2)

    def down(n, m):
        out[n] = m.reshape(2, P, D).transpose(1, 0, 2).reshape(P, SLOT)

    def halves(first):
        c = first + np.arange(4 * HEAD_DIM).reshape(2, 2, 2, HEAD_DIM // 2)
        return c.transpose(0, 2, 1, 3).ravel()

    for i, kind in enumerate(MIXERS):
        w_in, w_out = w[f"l{i}_w_in"], w[f"l{i}_w_out"]
        seen = {}
        for name, g, n, _, _ in SUBS[2 * i][1]:
            if name == "out":
                down(n, w_out[256 * g:256 * g + 256])
            elif kind == "dsa" and name == "misc":
                up(n, w_in[:, np.r_[1024:1088, 1664:1728, 1088:1152, 1728:1736]])
            elif kind == "dsa" and name == "qi":
                up(n, w_in[:, halves(1152 + 256 * g)])
            elif kind in ("dsa", "moba") and name in ("q", "k"):
                up(n, w_in[:, halves((0 if name == "q" else D) + 256 * g)])
            elif kind == "moba" and name == "v":
                up(n, w_in[:, 2 * D + 256 * g:2 * D + 256 * g + 256])
            elif kind == "ret" and name in ("q", "k", "rv", "rgate"):
                c = {"q": 0, "k": D, "rv": 2 * D, "rgate": 4 * D}[name] + 256 * g
                up(n, w_in[:, c:c + 256])
        first = SUBS[2 * i + 1][1][1][2]
        w_up, w_down = w[f"l{i}_w_up"], w[f"l{i}_w_down"]
        for s in range(STEPS):
            a, b, c = ffn_slots(first, s)
            up(a, w_up[:, 256 * s:256 * s + 256])
            up(b, w_up[:, D_FF + 256 * s:D_FF + 256 * s + 256])
            down(c, w_down[256 * s:256 * s + 256])
    return out


def lay_tables():
    def rope(dim):
        inv = (1.0 / (np.float32(10000.0) ** (np.arange(0, dim, 2, dtype=np.float32) / np.float32(dim)))).astype(np.float32)
        ang = (np.arange(SEQ, dtype=np.float32)[None, :] * inv[:, None]).astype(np.float32)
        rep = P // (dim // 2)
        return np.tile(np.cos(ang), (rep, 1)), np.tile(np.sin(ang), (rep, 1))

    att = np.zeros((P, TABLE), np.float32)
    att[:, 0:256], att[:, 256:512] = rope(HEAD_DIM)
    att[64:P, 256:512] *= -1
    for i in range(2):
        for r in range(P):
            if r // 32 % 2 == i:
                att[r, 1024 + i] = 1.0
                for u in range(2):
                    att[64 * u + 32 * (r // 64) + r % 32, 512 + P * (2 * u + i) + r] = 1.0
    ret = np.zeros((P, TABLE), np.float32)
    ret[:, 0:256], ret[:, 256:512] = rope(2 * P)
    key, query = np.arange(P)[:, None], np.arange(P)[None, :]
    for h in range(RET_HEADS):
        log_gamma = np.log1p(-(2.0 ** (-5.0 - h)))
        diag = np.where(query >= key, np.exp((query - key) * log_gamma), 0.0)
        across = np.exp((P + query - key) * log_gamma)
        ret[:, 512 + 256 * h:640 + 256 * h] = diag / 16
        ret[:, 640 + 256 * h:768 + 256 * h] = across / 16
    ident = np.eye(P, dtype=np.float32)
    causal = np.zeros((P, 3 * P), np.float32)
    late = np.where(np.arange(P)[None, :] > np.arange(P)[:, None], np.float32(NEG), np.float32(0))
    causal[:, 0:P] = late
    causal[:, 2 * P:3 * P] = late
    return np.stack([att, ret]), np.concatenate([ident, causal], axis=1)


def build(nc, x_in, xT_in, w_slots, ln_rows, conv_cols, gn_cols, tables, consts, out, n_subs=2 * DEPTH):
    n_slots = N_SLOTS if n_subs == 2 * DEPTH else SUBS[n_subs][1][0][2]

    with ExitStack() as ctx:
        def sb(name, shape, dt=F32):
            return ctx.enter_context(nc.sbuf_tensor(name, shape, dt))

        def sem(name):
            return ctx.enter_context(nc.semaphore(name))

        raw = sb("raw", [P, RAW, SLOT])
        w_hi = sb("w_hi", [P, RING, SLOT], F32R)
        w_lo = sb("w_lo", [P, RING, SLOT], F32R)
        xT_hi = sb("xT_hi", [P, KD, SEQ], F32R)
        xT_lo = sb("xT_lo", [P, KD, SEQ], F32R)
        x = sb("x", [P, TT, D])
        ln = sb("ln", [P, 2, D])
        act_hi = sb("act_hi", [P, 2, 2, SEQ], F32R)
        act_lo = sb("act_lo", [P, 2, 2, SEQ], F32R)
        mask_r = sb("mask_r", [P, 3 * P], F32R)
        ident_r = sb("ident_r", [P, P], F32R)
        table = sb("table", [P, TABLE])
        const = sb("const", [P, 4 * P])
        conv = sb("conv", [P, 2 * D_FF // P, 4])
        gn = sb("gn", [P, 16, 2])
        stat = sb("stat", [P, 96])
        scratch = sb("scratch", [P, 8704])

        ident = const[:, 0:P]
        causal = const[:, P:4 * P]
        cos = table[:, 0:SEQ]
        sin = table[:, SEQ:2 * SEQ]

        def piece(at, *shape):
            size = int(np.prod(shape))
            v = scratch[:, at:at + size]
            if len(shape) == 2:
                return v.rearrange("p (a b) -> p a b", b=shape[1])
            if len(shape) == 3:
                return v.rearrange("p (a b c) -> p a b c", b=shape[1], c=shape[2])
            return v

        first_xT = piece(0, KD, SEQ)
        xT_copy = piece(0, KD, P)
        taps = [[piece(1024 * b + 512 * u, 2, SEQ) for u in range(2)] for b in range(2)]
        gate = [piece(2048 + 512 * b, 2, SEQ) for b in range(2)]
        prod = [piece(3072 + 512 * b, 2, SEQ) for b in range(2)]
        by_cos = piece(0, 2, SEQ)
        by_sin = piece(512, 2, SEQ)
        qT = [piece(1024 + 512 * g, 2, SEQ) for g in range(4)]
        k_diag = piece(3072, 2, 2, SEQ)
        v = [piece(4096 + 512 * g, TT, 256) for g in range(2)]
        probs = piece(5120, 1536)
        probsT = piece(6656, 1536)
        ki_diag = piece(5120, 2, SEQ)
        relu = [piece(1024, 512), piece(1536, 512), piece(4608, 512)]
        index = piece(6144, 3 * P)
        left = piece(6528, 3 * P)
        narrow = piece(6912, SEQ)
        kT = [piece(3072 + 512 * g, 2, SEQ) for g in range(2)]
        ret_v = piece(4096, TT, 512)
        ret_gate = piece(5120, 4, SEQ)
        decayed = piece(6144, 3 * P)
        normed = piece(6656, TT, 512)
        scaled = [piece(2048 + 512 * b, 2, SEQ) for b in range(2)]
        ret_prod = [piece(7680 + 512 * b, 2, SEQ) for b in range(2)]

        acc = ctx.enter_context(nc.psum_tensor("acc", [P, TT, D], F32))
        work = ctx.enter_context(nc.psum_tensor("work", [P, TURNS, 512], F32))

        consts_in = sem("consts_in")
        gn_in = sem("gn_in")
        x_in_sem = sem("x_in_sem")
        xT_in_sem = sem("xT_in_sem")
        first_hi = sem("first_hi")
        first_lo = sem("first_lo")
        conv_in = sem("conv_in")
        ln_in = sem("ln_in")
        table_in = sem("table_in")
        raw_in = [sem(f"raw_in{r}") for r in range(RAW)]
        hi_ready = sem("hi_ready")
        lo_ready = sem("lo_ready")
        turn_full = [sem(f"turn_full{b}") for b in range(TURNS)]
        turn_read = [sem(f"turn_read{b}") for b in range(TURNS)]
        turn_half = sem("turn_half")
        pair_prod = sem("pair_prod")
        pair_hi = sem("pair_hi")
        pair_lo = sem("pair_lo")
        pair_used = sem("pair_used")
        acc_bank = sem("acc_bank")
        first_tap = sem("first_tap")
        second_tap = sem("second_tap")
        gate_ready = sem("gate_ready")
        var_ready = sem("var_ready")
        std_ready = sem("std_ready")
        x_ready = sem("x_ready")
        ident_ready = sem("ident_ready")
        roped = sem("roped")
        keys_summed = sem("keys_summed")
        wi_ready = sem("wi_ready")
        relu_ready = sem("relu_ready")
        relu_used = sem("relu_used")
        mask_ready = sem("mask_ready")
        max_ready = sem("max_ready")
        exp_done = sem("exp_done")
        probs_ready = sem("probs_ready")
        sums_inv = sem("sums_inv")
        scaled_ready = sem("scaled_ready")
        dve_step = sem("dve_step")
        out_done = sem("out_done")

        def at(base, it, per):
            return base if it is None else it * per + base

        release = {}
        pair_of_out = {}
        lo_event = {}
        proj_turn = {}
        for si, (kind, stages) in enumerate(SUBS):
            outs = [st for st in stages if st[0] in ("values", "ryT")]
            first_pair = outs[0][4] if outs else 0
            for name, g, n, k, p in stages:
                if name in ("q", "k", "v", "qi", "rv", "rgate"):
                    release[n] = ("turn", k)
                elif name == "misc":
                    release[n] = ("turn", k + 1)
                elif name == "out":
                    release[n] = ("pair", first_pair + g)
                elif name == "ffn":
                    for s in range(STEPS):
                        a, b, c = ffn_slots(n, s)
                        release[a] = ("turn", k + 2 * s)
                        release[b] = ("turn", k + 2 * s + 1)
                        release[c] = ("pair", p + s)
        last_pair = {}
        product_pairs = []
        p_end = 0
        for si, (kind, stages) in enumerate(SUBS):
            for name, g, n, k, p in stages:
                made = {"values": 1, "ryT": 2, "ffn": STEPS}.get(name, 0)
                if name != "values":
                    product_pairs += range(p_end, p_end + made)
                p_end += made
            last_pair[si] = p_end

        def products(p):
            return sum(1 for q in product_pairs if q <= p)

        def wait_full(eng, k, it=None):
            eng.wait_ge(turn_full[k % TURNS], at(k // TURNS + 1, it, 1))

        def wait_read(eng, k, it=None):
            eng.wait_ge(turn_read[k % TURNS], at(k // TURNS + 1, it, 1))

        def wait_slot_used(eng, n, it=None):
            what, i = release[n]
            if what == "turn":
                wait_full(eng, i, it)
            else:
                eng.wait_ge(pair_used, at(i + 1, it, 2))

        nth = {}
        ordinal = {}
        for si, (kind, stages) in enumerate(SUBS):
            for j, (name, g, n, k, p) in enumerate(stages):
                key = "rope" if name in ("q", "k", "qi") else name
                m = 2 if name == "spread" else 1
                key = "rope" if name == "spread" else key
                ordinal[si, j] = nth.get(key, 0)
                nth[key] = nth.get(key, 0) + m

        def dsa_count(si):
            return sum(1 for kind, _ in SUBS[:si + 1] if kind == "dsa")

        def mask_count(si):
            return sum(1 for kind, _ in SUBS[:si + 1] if kind in ("dsa", "moba"))

        def rope_needed(si, j):
            stages = SUBS[si][1]
            name, g = stages[j][:2]
            want = {"index": [("qi", g), ("spread", 0)], "scores": [("q", g), ("k", g), ("spread", 0)],
                    "rscores": [("q", g), ("k", g)]}[name]
            return max(ordinal[si, i] + (2 if st[0] == "spread" else 1)
                       for i, st in enumerate(stages) if (st[0], st[1]) in want)

        def find_turn(si, name, g):
            return next(st[3] for st in SUBS[si][1] if st[0] == name and st[1] == g)

        def v_turn(si, g):
            return find_turn(si, "misc", 0) + 1 if SUBS[si][0] == "dsa" else find_turn(si, "v", g)

        def rv_turn(si, g):
            return find_turn(si, "rv", g)

        def values_turn(si, g):
            return find_turn(si, "values", g)

        def var_count(what, si, g, t):
            n = sum(TT + (TT * RET_HEADS if kind == "ret" else 0) for kind, _ in SUBS[:si])
            if what == "ret":
                return n + TT * g + t + 1
            return n + (TT * RET_HEADS if SUBS[si][0] == "ret" else 0) + t + 1

        def ahead(si, j):
            name, g, n = SUBS[si][1][j][:3]
            early = {"moba": 1, "ret": 2}.get(SUBS[si][0], 0)
            first = SUBS[si][1][0][2]
            return min(n + 4, first + RING - 1) if early and n < first + early + 2 else n + 4

        def find_pair(si, h):
            return next(st[4] for st in SUBS[si][1] if st[0] == "ryT" and st[1] == h)

        subs = SUBS[:n_subs]
        block = ctx.enter_context(nc.Block())

        @block.sync
        def _(sp):
            sp.dma_start(first_xT[:, :, :].rearrange("p a b -> p (a b)"), xT_in).then_inc(xT_in_sem, 16)
            for n in range(RAW):
                sp.dma_start(raw[:, n, :], w_slots[n * P:(n + 1) * P, :]).then_inc(raw_in[n], 16)

            def load(n_here, row, r):
                sp.wait_ge(lo_ready, n_here)
                sp.dma_start(raw[:, r, :], w_slots[row, :]).then_inc(raw_in[r], 16)

            rounds = n_slots // RAW - 1
            with sp.Fori(0, rounds) as it:
                for r in range(RAW):
                    load(it * RAW + (r + 1), bass.ds(it * (RAW * P) + (RAW + r) * P, P), r)
            for n in range(RAW * (rounds + 1), n_slots):
                load(n - RAW + 1, bass.ds(n * P, P), n % RAW)
            for t in range(TT):
                for half in range(2):
                    sp.wait_ge(x_ready, 2 * TT * (n_subs - 1) + 2 * t + half + 1)
                    c = slice(512 * half, 512 * half + 512)
                    sp.dma_start(out[t * P:(t + 1) * P, c], x[:, t, c]).then_inc(out_done, 16)
            sp.wait_ge(out_done, 2 * 16 * TT)

        @block.tensor
        def _(pe):
            def mm(o, a, b, start, stop):
                return pe.matmul(o, a, b, start=start, stop=stop)

            def take_turn(k, it=None):
                if k >= TURNS or it is not None:
                    pe.wait_ge(turn_read[k % TURNS], at(k // TURNS, it, 1))

            def slot_in(n, it=None):
                pe.wait_ge(lo_ready, at(n + 1, it, RING))

            def up_hi(n, k, a, b):
                return w_hi[:, n % RING, 256 * k + a:256 * k + b]

            def up_lo(n, k, a, b):
                return w_lo[:, n % RING, 256 * k + a:256 * k + b]

            def to_features(n, o, a, b, tok=slice(0, SEQ)):
                for k in range(KD):
                    mm(o, up_hi(n, k, a, b), xT_hi[:, k, tok], k == 0, False)
                    mm(o, up_hi(n, k, a, b), xT_lo[:, k, tok], False, False)
                    last = mm(o, up_lo(n, k, a, b), xT_hi[:, k, tok], False, k == KD - 1)
                return last

            def to_tokens(n, o, t, a, b):
                tok = slice(t * P, (t + 1) * P)
                for k in range(KD):
                    mm(o, xT_hi[:, k, tok], up_hi(n, k, a, b), k == 0, False)
                    mm(o, xT_hi[:, k, tok], up_lo(n, k, a, b), False, False)
                    last = mm(o, xT_lo[:, k, tok], up_hi(n, k, a, b), False, k == KD - 1)
                return last

            def project(n, k, it=None):
                slot_in(n, it)
                take_turn(k, it)
                for j in range(2):
                    last = to_features(n, work[:, k % TURNS, j * SEQ:(j + 1) * SEQ], j * P, (j + 1) * P)
                last.then_inc(turn_full[k % TURNS], 1)

            def token_slot(n, k, cols, tiles):
                if 0 in tiles:
                    slot_in(n)
                    take_turn(k)
                for t in tiles:
                    last = to_tokens(n, work[:, k % TURNS, 256 * t:256 * t + cols.stop - cols.start], t, cols.start, cols.stop)
                if TT - 1 in tiles:
                    last.then_inc(turn_full[k % TURNS], 1)

            def key_slot(n, k):
                take_turn(k)
                to_features(n, work[:, k % TURNS, 0:SEQ], 0, P).then_inc(turn_full[k % TURNS], 1)

            def transpose_tile(si, k, t):
                for half in range(2):
                    pe.wait_ge(x_ready, 2 * TT * (si - 1) + 2 * t + half + 1)
                    kk = k + 2 * t + half
                    take_turn(kk)
                    for c in range(4):
                        f = (4 * half + c) * P
                        last = pe.transpose(work[:, kk % TURNS, c * P:(c + 1) * P], x[:, t, f:f + P], ident)
                    last.then_inc(turn_full[kk % TURNS], 1)

            def xT_in_place(k, t):
                wait_read(pe, k + 2 * t)
                wait_read(pe, k + 2 * t + 1)

            def start_sublayer(si, kind, stages):
                k = stages[0][3]
                if si == 0:
                    pe.wait_ge(first_lo, 2)
                    for _, cols, n, kk in early_slots(kind, stages):
                        token_slot(n, kk, cols, [0])
                    return
                transpose_tile(si, k, 0)
                if kind != "ffn":
                    xT_in_place(k, 0)
                    for _, cols, n, kk in early_slots(kind, stages):
                        token_slot(n, kk, cols, [0])
                transpose_tile(si, k, 1)
                for t in range(TT):
                    xT_in_place(k, t)

            def early_slots(kind, stages):
                names = {"dsa": ["misc"], "moba": ["v"], "ret": ["rv"]}[kind]
                return [(g, slice(P, P + 72) if kind == "dsa" else slice(0, 256), n, k + (kind == "dsa"))
                        for name, g, n, k, _ in stages if name in names and g < (2 if kind == "ret" else 1)]

            def accumulate(n, p, first, final, it=None):
                slot_in(n, it)
                for t in range(TT):
                    tok = slice(t * P, (t + 1) * P)
                    order = [(j, h) for h in range(2) for j in range(2)] if final else \
                        [(j, h) for j in range(2) for h in range(2)]
                    for j, half in order:
                        hi, lo = act_hi[:, p % 2, j, tok], act_lo[:, p % 2, j, tok]
                        c = j * D + half * HALVES
                        wh = w_hi[:, n % RING, c:c + HALVES]
                        wl = w_lo[:, n % RING, c:c + HALVES]
                        o = acc[:, t, half * HALVES:(half + 1) * HALVES]
                        mm(o, hi, wh, first and j == 0, False)
                        mm(o, hi, wl, False, False)
                        last = mm(o, lo, wh, False, final and j == 1)
                        if final and j == 1 and (t, half) != (1, 1):
                            last.then_inc(acc_bank, 1)
                last.then_inc(pair_used, 1)

            def ffn(n0, k0, p0):
                def step(s, it=None):
                    a, b, _ = ffn_slots(n0, s)
                    project(a, k0 + 2 * s, it)
                    project(b, k0 + 2 * s + 1, it)
                    if s:
                        pe.wait_ge(pair_lo, at(products(p0 + s - 1), it, 2))
                        accumulate(b + 1, p0 + s - 1, s == 1 and it is None, False, it)

                step(0)
                step(1)
                with pe.Fori(0, (STEPS - 3) // 2) as it:
                    step(2, it)
                    step(3, it)
                step(STEPS - 1)
                pe.wait_ge(pair_lo, products(p0 + STEPS - 1))
                accumulate(n0 + 3 * STEPS - 1, p0 + STEPS - 1, False, True)

            pe.wait_ge(consts_in, 16)
            pe.wait_ge(ident_ready, 1)
            for si, (kind, stages) in enumerate(subs):
                for j, (name, g, n, k, p) in enumerate(stages):
                    if name == "xT":
                        start_sublayer(si, kind, stages)
                    elif name == "ffn":
                        ffn(n, k, p)
                    elif name == "misc":
                        key_slot(n, k)
                        token_slot(n, k + 1, slice(P, P + 72), [1])
                    elif name in ("q", "k", "qi", "rgate"):
                        project(n, k)
                    elif name in ("v", "rv"):
                        started = g < (2 if kind == "ret" else 1)
                        token_slot(n, k, slice(0, 256), [1] if started else [0, 1])
                    elif name == "spread":
                        wait_read(pe, k - 2)
                        pe.wait_ge(table_in, 16 * (si // 2 + 1))
                        for u in range(2):
                            take_turn(k + u)
                            for half in range(2):
                                sel = table[:, 512 + P * (2 * u + half):512 + P * (2 * u + half + 1)]
                                last = mm(work[:, (k + u) % TURNS, half * SEQ:(half + 1) * SEQ], sel, narrow, True, True)
                            last.then_inc(turn_full[(k + u) % TURNS], 1)
                    elif name in ("scores", "index"):
                        pe.wait_ge(roped, rope_needed(si, j))
                        if name == "scores":
                            pe.wait_ge(mask_ready, mask_count(si))
                            qs = qT[g if kind == "dsa" else g % 2]
                        else:
                            qs = qT[2 + g]
                        for part in range(3):
                            b = (k + part) % TURNS
                            take_turn(k + part)
                            keys = P if part == 0 else SEQ
                            heads = range(4) if part == 0 else range(2 * part - 2, 2 * part)
                            q0 = 0 if part == 0 else P
                            o = work[:, b, :].rearrange("p (h k) -> p h k", k=keys)
                            if name == "scores":
                                m = mask_r[:, 0:P] if part == 0 else mask_r[:, P:3 * P]
                                mm(o, ident_r[:, :], m.unsqueeze(1).to_broadcast([P, len(heads), keys]), True, False)
                            for u in ((0, 1) if part == 0 else (part - 1,)):
                                dst = o[:, 2 * u:2 * u + 2, :] if part == 0 else o
                                ks = ki_diag if name == "index" else k_diag[:, 0 if kind == "dsa" else u, :, :]
                                last = mm(dst, qs[:, u, q0:q0 + P], ks[:, :, 0:keys], name == "index",
                                          name == "index" or u == 1 or part > 0)
                            last.then_inc(turn_full[b], 1)
                    elif name == "probsT":
                        for part in range(3):
                            b = (k + part) % TURNS
                            take_turn(k + part)
                            pe.wait_ge(probs_ready, 3 * ordinal[si, j] + part + 1)
                            for c in range(4):
                                last = pe.transpose(work[:, b, c * P:(c + 1) * P],
                                                    probs[:, 512 * part + c * P:512 * part + (c + 1) * P], ident)
                            last.then_inc(turn_full[b], 1)
                    elif name == "values":
                        for part in range(3):
                            wait_read(pe, k - 3 + part)
                        wait_read(pe, v_turn(si, g))
                        take_turn(k)
                        for h in range(4):
                            vh = (lambda t: v[0][:, t, 0:HEAD_DIM]) if kind == "dsa" else \
                                (lambda t: v[g % 2][:, t, h * HEAD_DIM:(h + 1) * HEAD_DIM])
                            rows = slice(64 * (h % 2), 64 * (h % 2) + 64)
                            o = work[rows, k % TURNS, :]
                            c0 = (h // 2) * SEQ
                            mm(o[:, c0:c0 + P], vh(0), probsT[:, h * P:(h + 1) * P], True, True)
                            late = 512 + h * SEQ
                            mm(o[:, c0 + P:c0 + SEQ], vh(0), probsT[:, late:late + P], True, False)
                            last = mm(o[:, c0 + P:c0 + SEQ], vh(1), probsT[:, late + P:late + SEQ], False, True)
                        last.then_inc(turn_full[k % TURNS], 1)
                    elif name == "out":
                        _, pp = release[n]
                        first = g == 0
                        final = j == len(stages) - 1
                        if kind == "ret":
                            pe.wait_ge(pair_lo, products(pp))
                        else:
                            wait_read(pe, values_turn(si, g))
                        accumulate(n, pp, first, final)
                    elif name == "rscores":
                        pe.wait_ge(roped, rope_needed(si, j))
                        take_turn(k)
                        b = k % TURNS
                        for d in range(2):
                            mm(work[:, b, 0:SEQ], kT[g % 2][:, d, 0:P], qT[g % 2][:, d, :], d == 0, d == 1)
                        for d in range(2):
                            last = mm(work[:, b, SEQ:SEQ + P], kT[g % 2][:, d, P:SEQ], qT[g % 2][:, d, P:SEQ],
                                      d == 0, d == 1)
                        last.then_inc(turn_full[b], 1)
                    elif name == "rvalues":
                        wait_read(pe, find_turn(si, "rscores", g))
                        for u in range(2):
                            wait_read(pe, rv_turn(si, 2 * g + u))
                        take_turn(k)
                        mm(work[:, k % TURNS, :], decayed[:, 0:P], ret_v[:, 0, :], True, True)\
                            .then_inc(turn_full[k % TURNS], 1)
                        take_turn(k + 1)
                        o = work[:, (k + 1) % TURNS, :]
                        mm(o, decayed[:, P:2 * P], ret_v[:, 0, :], True, False)
                        mm(o, decayed[:, 2 * P:3 * P], ret_v[:, 1, :], False, True)\
                            .then_inc(turn_full[(k + 1) % TURNS], 1)
                    elif name == "ryT":
                        for t in range(TT):
                            wait_read(pe, find_turn(si, "rvalues", g) + t)
                        for u in range(2):
                            b = (k + u) % TURNS
                            take_turn(k + u)
                            for c in range(2):
                                for t in range(TT):
                                    f = (2 * u + c) * P
                                    last = pe.transpose(work[:, b, c * SEQ + t * P:c * SEQ + (t + 1) * P],
                                                        normed[:, t, f:f + P], ident)
                            last.then_inc(turn_full[b], 1)

        @block.scalar
        def _(act):
            fed = [0]

            def split_hi(n, it=None):
                act.wait_ge(raw_in[n % RAW], at(16 * (n // RAW + 1), it, 16 * (RING // RAW)))
                if n >= RING:
                    wait_slot_used(act, n - RING, it)
                act.activation(w_hi[:, n % RING, :], raw[:, n % RAW, :], ACT.Copy).then_inc(hi_ready, 1)

            def feed(upto):
                while fed[0] < min(upto + 1, n_slots):
                    split_hi(fed[0])
                    fed[0] += 1

            def ffn(n0, k0, p0, layer):
                def step(s, it=None):
                    a = ffn_slots(n0, s)[0]

                    def feed_one(i):
                        if it is not None:
                            split_hi(a + 3 + i, it)
                        else:
                            feed(a + 3 + i if s else a + 2 + i)

                    b = (p0 + s) % 2
                    for u in range(2):
                        k = k0 + 2 * s + u
                        if u == 0 and s >= 2:
                            act.wait_ge(pair_prod, at(products(p0 + s - 2), it, 2))
                        wait_full(act, k, it)
                        for j in range(2):
                            last = conv_col(b, u, j, k, s, it)
                        last.then_inc(first_tap, 1)
                        feed_one(u)
                    wait_read(act, k0 + 2 * s, it)
                    act.activation(gate[b][:, :, :], taps[b][0][:, :, :], ACT.Silu).then_inc(gate_ready, 1)
                    feed_one(2)
                    act.wait_ge(pair_prod, at(products(p0 + s), it, 2))
                    act.wait_ge(pair_used, at(p0 + s - 1, it, 2))
                    act.activation(act_hi[:, b, :, :], prod[b][:, :, :], ACT.Copy).then_inc(pair_hi, 1)

                def conv_col(b, u, j, k, s, it):
                    c = 2 * s + j + u * (D_FF // P)
                    if it is None:
                        w2, bias = conv[:, c, 2:3], conv[:, c, 3:4]
                    else:
                        w2 = conv[:, bass.ds(it * 4 + c, 1), 2:3].rearrange("p a b -> p (a b)")
                        bias = conv[:, bass.ds(it * 4 + c, 1), 3:4].rearrange("p a b -> p (a b)")
                    return act.activation(taps[b][u][:, j, :], work[:, k % TURNS, j * SEQ:(j + 1) * SEQ],
                                          ACT.Identity, bias=bias, scale=w2)

                act.wait_ge(conv_in, 16 * (layer + 1))
                step(0)
                step(1)
                with act.Fori(0, (STEPS - 3) // 2) as it:
                    step(2, it)
                    step(3, it)
                fed[0] = ffn_slots(n0, STEPS - 1)[0] + 3
                step(STEPS - 1)

            act.wait_ge(xT_in_sem, 16)
            for half in range(2):
                act.activation(xT_hi[:, 4 * half:4 * half + 4, :], first_xT[:, 4 * half:4 * half + 4, :], ACT.Copy)\
                    .then_inc(first_hi, 1)
            feed(0)
            act.wait_ge(consts_in, 16)
            act.activation(ident_r[:, :], ident, ACT.Copy).then_inc(ident_ready, 1)
            feed(3)
            for si, (kind, stages) in enumerate(subs):
                for j, (name, g, n, k, p) in enumerate(stages):
                    if name in ("q", "k", "qi", "v", "rv", "rgate", "misc", "out"):
                        feed(ahead(si, j))
                    if name == "ffn":
                        ffn(n, k, p, si // 2)
                    elif name == "misc":
                        wait_full(act, k)
                        act.activation(narrow, work[:, k % TURNS, 0:SEQ], ACT.Copy).then_inc(turn_read[k % TURNS], 1)
                        wait_full(act, k + 1)
                        o = work[:, (k + 1) % TURNS, :].rearrange("p (t c) -> p t c", t=2)
                        act.activation(stat[:, 64:64 + 16].rearrange("p (t h) -> p t h", t=2), o[:, :, 64:72], ACT.Copy,
                                       scale=IDX_SCALE).then_inc(wi_ready, 1)
                        act.activation(v[0][:, :, 0:HEAD_DIM], o[:, :, 0:HEAD_DIM], ACT.Copy)\
                            .then_inc(turn_read[(k + 1) % TURNS], 1)
                    elif name in ("v", "rv"):
                        wait_full(act, k)
                        o = work[:, k % TURNS, :].rearrange("p (t c) -> p t c", t=2)
                        dst = v[g % 2][:, :, :] if name == "v" else ret_v[:, :, 256 * (g % 2):256 * (g % 2) + 256]
                        act.activation(dst, o, ACT.Copy).then_inc(turn_read[k % TURNS], 1)
                    elif name == "index":
                        for part in range(3):
                            i = 3 * ordinal[si, j] + part
                            wait_full(act, k + part)
                            if i >= 3:
                                act.wait_ge(relu_used, i - 2)
                            act.activation(relu[part], work[:, (k + part) % TURNS, :], ACT.Relu)\
                                .then_inc(turn_read[(k + part) % TURNS], 1)
                    elif name == "scores":
                        o0 = ordinal[si, j]
                        if g:
                            wait_full(act, find_turn(si, "probsT", g - 1) + 2)
                        for part in range(3):
                            i = 3 * o0 + part
                            act.wait_ge(max_ready, i + 1)
                            keys = P if part == 0 else SEQ
                            heads = 4 if part == 0 else 2
                            c0 = 0 if part == 0 else 2 + 2 * part
                            for h in range(heads):
                                c = c0 + h
                                ins = act.activation(probs[:, 512 * part + h * keys:512 * part + (h + 1) * keys],
                                                     work[:, (k + part) % TURNS, h * keys:(h + 1) * keys], ACT.Exp,
                                                     bias=stat[:, 16 + c:17 + c], scale=SCALE,
                                                     accum_out=stat[:, 24 + c:25 + c])
                            ins.then_inc(turn_read[(k + part) % TURNS], 1)
                    elif name == "probsT":
                        if g:
                            wait_full(act, find_turn(si, "values", g - 1))
                        for part in (0, 2):
                            wait_full(act, k + part)
                            act.activation(probsT[:, 512 * part:512 * part + 512], work[:, (k + part) % TURNS, :], ACT.Copy)\
                                .then_inc(turn_read[(k + part) % TURNS], 1)
                    elif name == "values":
                        wait_full(act, k)
                        if p >= 2:
                            act.wait_ge(pair_used, p - 1)
                        act.activation(act_hi[:, p % 2, :, :], work[:, k % TURNS, :].rearrange("p (c t) -> p c t", c=2),
                                       ACT.Copy).then_inc(pair_hi, 1)
                    elif name == "rgate":
                        if g >= 2 and g % 2 == 0:
                            act.wait_ge(pair_prod, products(find_pair(si, g // 2 - 1) + 1))
                        wait_full(act, k)
                        act.activation(ret_gate[:, 2 * (g % 2):2 * (g % 2) + 2, :],
                                       work[:, k % TURNS, :].rearrange("p (c t) -> p c t", c=2), ACT.Silu)\
                            .then_inc(turn_read[k % TURNS], 1)
                    elif name == "rvalues":
                        for t in range(TT):
                            c = 2 * t
                            i = var_count("ret", si, g, t)
                            act.wait_ge(var_ready, i)
                            act.activation(stat[:, 80 + t:81 + t], stat[:, 40 + c + 1:42 + c], ACT.Sqrt,
                                           bias=stat[:, 95:96]).then_inc(std_ready, 1)
                    elif name == "ryT":
                        act.wait_ge(gn_in, 16)
                        for u in range(2):
                            wait_full(act, k + u)
                            pp = p + u
                            act.wait_ge(pair_prod, products(pp - 2))
                            for c in range(2):
                                col = 4 * g + 2 * u + c
                                ins = act.activation(scaled[u][:, c, :], work[:, (k + u) % TURNS, c * SEQ:(c + 1) * SEQ],
                                                     ACT.Identity, bias=gn[:, col, 1:2], scale=gn[:, col, 0:1])
                            ins.then_inc(turn_read[(k + u) % TURNS], 1)
                        for u in range(2):
                            pp = p + u
                            act.wait_ge(pair_prod, products(pp))
                            act.wait_ge(pair_used, pp - 1)
                            act.activation(act_hi[:, pp % 2, :, :], ret_prod[u][:, :, :], ACT.Copy).then_inc(pair_hi, 1)
                act.activation(stat[:, 92:93], stat[:, 94:95], ACT.Sqrt)
                for t in range(TT):
                    act.wait_ge(var_ready, var_count("ln", si, 0, t))
                    act.activation(stat[:, 4 + t:5 + t], stat[:, 2 * t + 1:2 * t + 2], ACT.Sqrt,
                                   bias=stat[:, 94:95]).then_inc(std_ready, 1)
                    if si + 1 < n_subs:
                        k = SUBS[si + 1][1][0][3]
                        for half in range(2):
                            kk = k + 2 * t + half
                            wait_full(act, kk)
                            if t == 0:
                                act.activation(xT_copy[:, 4 * half:4 * half + 4, :],
                                               work[:, kk % TURNS, :].rearrange("p (c t) -> p c t", c=4), ACT.Copy)
                            act.activation(xT_hi[:, 4 * half:4 * half + 4, t * P:(t + 1) * P],
                                           work[:, kk % TURNS, :].rearrange("p (c t) -> p c t", c=4), ACT.Copy)\
                                .then_inc(turn_half, 1)

        def xT_rest(eng, si, t, half):
            kk = SUBS[si + 1][1][0][3] + 2 * t + half
            eng.wait_ge(turn_half, 4 * si + 2 * t + half + 1)
            dst = (slice(None), slice(4 * half, 4 * half + 4), slice(t * P, (t + 1) * P))
            src = work[:, kk % TURNS, :].rearrange("p (c t) -> p c t", c=4) if t else xT_copy[:, 4 * half:4 * half + 4, :]
            eng.tensor_tensor(xT_lo[dst], src, xT_hi[dst], ALU.subtract).then_inc(turn_read[kk % TURNS], 1)

        @block.vector
        def _(dve):
            fed = [0]
            steps = [0]

            def settle(ins):
                steps[0] += 1
                ins.then_inc(dve_step, 1)
                dve.wait_ge(dve_step, steps[0])

            def split_lo(n, it=None):
                dve.wait_ge(hi_ready, at(n + 1, it, RING))
                dve.tensor_tensor(w_lo[:, n % RING, :], raw[:, n % RAW, :], w_hi[:, n % RING, :], ALU.subtract)\
                    .then_inc(lo_ready, 1)

            def feed(upto):
                while fed[0] < min(upto + 1, n_slots):
                    split_lo(fed[0])
                    fed[0] += 1

            def ffn(n0, k0, p0, layer):
                def col(s, u, j, tap, it):
                    c = 2 * s + j + u * (D_FF // P)
                    if it is None:
                        return conv[:, c, tap:tap + 1]
                    return conv[:, bass.ds(it * 4 + c, 1), tap:tap + 1].rearrange("p a b -> p (a b)")

                def step(s, it=None):
                    a = ffn_slots(n0, s)[0]
                    b = (p0 + s) % 2

                    def feed_one(i):
                        if it is not None:
                            split_lo(a + 3 + i, it)
                        else:
                            feed(a + 3 + i if s else a + 2 + i)

                    for u in range(2):
                        k = k0 + 2 * s + u
                        i = 2 * (STEPS * layer + s) + u
                        dve.wait_ge(first_tap, at(i + 1, it, 4))
                        for j in range(2):
                            o, h = taps[b][u][:, j, :], work[:, k % TURNS, j * SEQ:(j + 1) * SEQ]
                            ins = dve.scalar_tensor_tensor(out=o[:, 1:SEQ], in0=h[:, 0:SEQ - 1], scalar=col(s, u, j, 1, it),
                                                           in1=o[:, 1:SEQ], op0=ALU.mult, op1=ALU.add)
                        ins.then_inc(second_tap, 1)
                        dve.wait_ge(second_tap, at(i + 1, it, 4))
                        for j in range(2):
                            o, h = taps[b][u][:, j, :], work[:, k % TURNS, j * SEQ:(j + 1) * SEQ]
                            ins = dve.scalar_tensor_tensor(out=o[:, 2:SEQ], in0=h[:, 0:SEQ - 2], scalar=col(s, u, j, 0, it),
                                                           in1=o[:, 2:SEQ], op0=ALU.mult, op1=ALU.add)
                        ins.then_inc(turn_read[k % TURNS], 1)
                        feed_one(u)
                    feed_one(2)
                    dve.wait_ge(gate_ready, at(STEPS * layer + s + 1, it, 2))
                    wait_read(dve, k0 + 2 * s + 1, it)
                    dve.wait_ge(pair_lo, at(products(p0 + s - 2), it, 2)) if products(p0 + s - 2) else None
                    dve.tensor_tensor(prod[b][:, :, :], gate[b][:, :, :], taps[b][1][:, :, :], ALU.mult)\
                        .then_inc(pair_prod, 1)

                step(0)
                step(1)
                with dve.Fori(0, (STEPS - 3) // 2) as it:
                    step(2, it)
                    step(3, it)
                fed[0] = ffn_slots(n0, STEPS - 1)[0] + 3
                step(STEPS - 1)

            def norm(si):
                def add_residual(t):
                    for h in range(2):
                        if (t, h) == (1, 1):
                            dve.wait_ge(pair_used, last_pair[si])
                        else:
                            dve.wait_ge(acc_bank, 3 * si + 2 * t + h + 1)
                        c = slice(512 * h, 512 * h + 512)
                        settle(dve.scalar_tensor_tensor(out=x[:, t, c], in0=x[:, t, c], scalar=float(ALPHA),
                                                        in1=acc[:, t, c], op0=ALU.mult, op1=ALU.add))
                        ins = dve.bn_stats(stat[:, 48 + 6 * h:54 + 6 * h], x[:, t, c])
                    settle(ins)

                def normalize(t):
                    n = var_count("ln", si, 0, t)
                    dve.bn_aggr(stat[:, 2 * t:2 * t + 2], stat[:, 48:60]).then_inc(var_ready, 1)
                    dve.wait_ge(var_ready, n)
                    settle(dve.scalar_tensor_tensor(out=x[:, t, :], in0=x[:, t, :], scalar=stat[:, 2 * t:2 * t + 1],
                                                    in1=ln[:, 0, :], op0=ALU.subtract, op1=ALU.mult))
                    dve.wait_ge(std_ready, n)
                    settle(dve.reciprocal(stat[:, 6 + t:7 + t], stat[:, 4 + t:5 + t]))
                    for h in range(2):
                        c = slice(512 * h, 512 * h + 512)
                        dve.scalar_tensor_tensor(out=x[:, t, c], in0=x[:, t, c], scalar=stat[:, 6 + t:7 + t],
                                                 in1=ln[:, 1, c], op0=ALU.mult, op1=ALU.add).then_inc(x_ready, 1)

                dve.wait_ge(ln_in, 16 * (si + 1))
                if si == 0:
                    dve.wait_ge(x_in_sem, 16 * TT)
                for t in range(TT):
                    add_residual(t)
                    normalize(t)
                if si + 1 < n_subs:
                    for half in range(2):
                        xT_rest(dve, si, 1, half)

            def rotate(k, r, table_n, in_rows):
                wait_full(dve, k)
                dve.wait_ge(table_in, 16 * table_n)
                if r:
                    dve.wait_ge(roped, r)
                src = work[:, k % TURNS, :].rearrange("p (c t) -> p c t", c=2)
                dve.tensor_tensor(by_cos[:, :, :], src, cos.unsqueeze(1).to_broadcast([P, 2, SEQ]), ALU.mult)
                for to, rows in ((64, slice(0, 64)), (0, slice(64, P))) if in_rows else ((0, slice(0, P)),):
                    last = dve.tensor_tensor(by_sin[to:to + (rows.stop - rows.start), :, :], src[rows, :, :],
                                             sin[rows, :].unsqueeze(1).to_broadcast([rows.stop - rows.start, 2, SEQ]), ALU.mult)
                last.then_inc(turn_read[k % TURNS], 1)

            def topk(first, keys, rounds):
                for r in rounds:
                    src = index if r == 0 else left
                    settle(dve.max(stat[:, 84:92], src[:, first:first + keys]))
                    settle(dve.match_replace(left[:, first:first + keys], stat[:, 84:92], src[:, first:first + keys], TAKEN))

            dve.memset(stat[:, 94:95], LN_EPS)
            settle(dve.memset(stat[:, 95:96], GN_EPS))
            for half in range(2):
                c = slice(4 * half, 4 * half + 4)
                dve.wait_ge(first_hi, half + 1)
                dve.tensor_tensor(xT_lo[:, c, :], first_xT[:, c, :], xT_hi[:, c, :], ALU.subtract).then_inc(first_lo, 1)
            feed(3)
            dve.wait_ge(consts_in, 16)
            for si, (kind, stages) in enumerate(subs):
                for j, (name, g, n, k, p) in enumerate(stages):
                    if name in ("q", "k", "qi", "v", "rv", "rgate", "misc", "out"):
                        feed(ahead(si, j))
                    if name == "ffn":
                        ffn(n, k, p, si // 2)
                    elif name == "spread":
                        for u in range(2):
                            rotate(k + u, ordinal[si, j] + u, si // 2 + 1, True)
                    elif name in ("q", "k", "qi"):
                        rotate(k, ordinal[si, j], si // 2 + 1, kind != "ret")
                    elif name == "index":
                        if g == 0:
                            dve.wait_ge(wi_ready, dsa_count(si))
                        for part in range(3):
                            i = 3 * ordinal[si, j] + part
                            wait_read(dve, k + part)
                            heads = range(4) if part == 0 else range(2 * part - 2, 2 * part)
                            t = 0 if part == 0 else 1
                            dst = index[:, 0:P] if part == 0 else index[:, P:3 * P]
                            base = causal[:, 0:P] if part == 0 else causal[:, P:3 * P]
                            keys = P if part == 0 else SEQ
                            for m, h in enumerate(heads):
                                start = g == 0 and h == 0
                                ins = dve.scalar_tensor_tensor(
                                    out=dst, in0=relu[part][:, m * keys:(m + 1) * keys],
                                    scalar=stat[:, 64 + 8 * t + 4 * g + h:65 + 8 * t + 4 * g + h],
                                    in1=base if start else dst, op0=ALU.mult, op1=ALU.add)
                                if m < len(heads) - 1:
                                    settle(ins)
                            ins.then_inc(relu_used, 1)
                            dve.wait_ge(relu_used, i + 1)
                    elif name == "topk":
                        half = TOPK // 16
                        if g == 0:
                            topk(0, P, range(TOPK // 8))
                        elif g == 1:
                            topk(P, SEQ, range(half))
                        elif g == 2:
                            topk(P, SEQ, range(half, TOPK // 8))
                            settle(dve.tensor_scalar(index, left, TAKEN / 2, NEG, ALU.is_ge, ALU.mult))
                            dve.tensor_tensor(mask_r[:, :], index, causal, ALU.add).then_inc(mask_ready, 1)
                    elif name == "mask":
                        dve.tensor_copy(mask_r[:, :], causal).then_inc(mask_ready, 1)
                    elif name == "scores":
                        for part in range(3):
                            wait_full(dve, k + part)
                            keys = P if part == 0 else SEQ
                            heads = 4 if part == 0 else 2
                            c0 = 0 if part == 0 else 2 + 2 * part
                            settle(dve.tensor_reduce(stat[:, 8 + c0:8 + c0 + heads],
                                                     work[:, (k + part) % TURNS, :].rearrange("p (h k) -> p h k", k=keys),
                                                     AX_X, ALU.max))
                            dve.tensor_scalar(stat[:, 16 + c0:16 + c0 + heads], stat[:, 8 + c0:8 + c0 + heads],
                                              -SCALE, None, ALU.mult).then_inc(max_ready, 1)
                        for part in range(3):
                            wait_read(dve, k + part)
                            heads = 4 if part == 0 else 2
                            c0 = 0 if part == 0 else 2 + 2 * part
                            dve.reciprocal(stat[:, 32 + c0:32 + c0 + heads], stat[:, 24 + c0:24 + c0 + heads])\
                                .then_inc(sums_inv, 1)
                    elif name == "probsT":
                        wait_full(dve, k + 1)
                        if g:
                            wait_full(dve, find_turn(si, "values", g - 1))
                        dve.tensor_copy(probsT[:, 512:1024], work[:, (k + 1) % TURNS, :])\
                            .then_inc(turn_read[(k + 1) % TURNS], 1)
                    elif name == "values":
                        dve.wait_ge(pair_hi, p + 1)
                        dve.tensor_tensor(act_lo[:, p % 2, :, :], work[:, k % TURNS, :].rearrange("p (c t) -> p c t", c=2),
                                          act_hi[:, p % 2, :, :], ALU.subtract).then_inc(turn_read[k % TURNS], 1)
                    elif name == "rscores":
                        wait_full(dve, k)
                        o = work[:, k % TURNS, :]
                        d0 = 512 + 256 * g
                        dve.tensor_tensor(decayed[:, 0:SEQ], o[:, 0:SEQ], table[:, d0:d0 + SEQ], ALU.mult)
                        dve.tensor_tensor(decayed[:, SEQ:SEQ + P], o[:, SEQ:SEQ + P], table[:, d0:d0 + P], ALU.mult)\
                            .then_inc(turn_read[k % TURNS], 1)
                    elif name == "rvalues":
                        for t in range(TT):
                            o = work[:, (k + t) % TURNS, :]
                            wait_full(dve, k + t)
                            settle(dve.bn_stats(stat[:, 48 + 6 * t:54 + 6 * t], o))
                            dve.bn_aggr(stat[:, 40 + 2 * t:42 + 2 * t], stat[:, 48 + 6 * t:54 + 6 * t]).then_inc(var_ready, 1)
                        if g:
                            wait_full(dve, find_turn(si, "ryT", g - 1) + 1)
                        for t in range(TT):
                            o = work[:, (k + t) % TURNS, :]
                            dve.wait_ge(std_ready, var_count("ret", si, g, t))
                            settle(dve.reciprocal(stat[:, 82 + t:83 + t], stat[:, 80 + t:81 + t]))
                            dve.tensor_scalar(normed[:, t, :], o, stat[:, 40 + 2 * t:41 + 2 * t], stat[:, 82 + t:83 + t],
                                              ALU.subtract, ALU.mult).then_inc(turn_read[(k + t) % TURNS], 1)
                    elif name == "ryT":
                        for u in range(2):
                            pp = p + u
                            wait_read(dve, k + u)
                            dve.wait_ge(pair_lo, products(pp - 2))
                            dve.tensor_tensor(ret_prod[u][:, :, :], scaled[u][:, :, :], ret_gate[:, 2 * u:2 * u + 2, :],
                                              ALU.mult).then_inc(pair_prod, 1)
                norm(si)

        @block.gpsimd
        def _(pool):
            def load_ln(si):
                pool.dma_start(ln[:, :, :].rearrange("p a d -> p (a d)"), ln_rows[si, :].partition_broadcast(P))\
                    .then_inc(ln_in, 16)

            def load_table(i):
                pool.dma_start(table[:, :], tables[P * (MIXERS[i] == "ret"):P * (MIXERS[i] == "ret") + P, :])\
                    .then_inc(table_in, 16)

            def load_conv(i):
                pool.dma_start(conv[:, :, :].rearrange("p a b -> p (a b)"), conv_cols[P * i:P * (i + 1), :])\
                    .then_inc(conv_in, 16)

            pool.dma_start(const[:, :], consts).then_inc(consts_in, 16)
            pool.wait_ge(raw_in[0], 16)
            load_table(0)
            load_conv(0)
            for t in range(TT):
                pool.dma_start(x[:, t, :], x_in[t * P:(t + 1) * P, :]).then_inc(x_in_sem, 16)
            load_ln(0)
            pool.dma_start(gn[:, :, :].rearrange("p a b -> p (a b)"), gn_cols).then_inc(gn_in, 16)

            def rest(p, src, it=None):
                pool.wait_ge(pair_hi, at(p + 1, it, 2))
                pool.tensor_tensor(act_lo[:, p % 2, :, :], src[:, :, :], act_hi[:, p % 2, :, :], ALU.subtract)\
                    .then_inc(pair_lo, 1)

            for si, (kind, stages) in enumerate(subs):
                for j, (name, g, n, k, p) in enumerate(stages):
                    if name in ("q", "k", "qi", "spread"):
                        for u in range(2 if name == "spread" else 1):
                            r = ordinal[si, j] + u
                            wait_read(pool, k + u)
                            if kind == "ret":
                                dst = (kT if name == "k" else qT)[g % 2]
                                pool.tensor_tensor(dst[:, 0, :], by_cos[:, 0, :], by_sin[:, 1, :], ALU.subtract)
                                last = pool.tensor_tensor(dst[:, 1, :], by_cos[:, 1, :], by_sin[:, 0, :], ALU.add)
                            elif name == "k":
                                pool.tensor_tensor(by_cos[:, :, :], by_cos[:, :, :], by_sin[:, :, :], ALU.add)\
                                    .then_inc(keys_summed, 1)
                                pool.wait_ge(keys_summed, g + 1)
                                for i in range(2):
                                    block = table[:, 1024 + i:1025 + i].unsqueeze(1).to_broadcast([P, 2, SEQ])
                                    last = pool.tensor_tensor(k_diag[:, :, i, :], by_cos[:, :, :], block, ALU.mult)
                            else:
                                dst = (k_diag[:, 0, :, :], ki_diag)[u] if name == "spread" else \
                                    qT[2 + g] if name == "qi" else qT[g if kind == "dsa" else g % 2]
                                last = pool.tensor_tensor(dst[:, :, :], by_cos[:, :, :], by_sin[:, :, :], ALU.add)
                            last.then_inc(roped, 1)
                    elif name == "scores":
                        for part in range(3):
                            i = 3 * ordinal[si, j] + part
                            keys = P if part == 0 else SEQ
                            heads = 4 if part == 0 else 2
                            c0 = 0 if part == 0 else 2 + 2 * part
                            pool.wait_ge(sums_inv, i + 1)
                            pr = probs[:, 512 * part:512 * part + 512].rearrange("p (h k) -> p h k", k=keys)
                            pool.tensor_tensor(pr, pr, stat[:, 32 + c0:32 + c0 + heads].unsqueeze(2)
                                               .to_broadcast([P, heads, keys]), ALU.mult).then_inc(probs_ready, 1)
                    elif name == "ryT":
                        for u in range(2):
                            rest(p + u, ret_prod[u])
                    elif name == "ffn":
                        rest(p, prod[p % 2])
                        rest(p + 1, prod[(p + 1) % 2])
                        with pool.Fori(0, (STEPS - 3) // 2) as it:
                            rest(p + 2, prod[p % 2], it)
                            rest(p + 3, prod[(p + 1) % 2], it)
                        rest(p + STEPS - 1, prod[(p + STEPS - 1) % 2])
                if si + 1 < n_subs:
                    for half in range(2):
                        xT_rest(pool, si, 0, half)
                    pool.wait_ge(x_ready, 2 * TT * (si + 1))
                    load_ln(si + 1)
                    if si % 2:
                        load_conv(si // 2 + 1)
                    elif si // 2 + 1 < DEPTH:
                        load_table(si // 2 + 1)


def kernel(**inputs):
    import concourse.bacc as bacc
    from concourse.bass_utils import run_bass_kernel_spmd as run

    w = {k: np.asarray(a) for k, a in inputs.items()}
    tables, consts = lay_tables()
    conv_cols = np.concatenate([np.concatenate([w[f"l{i}_conv_w"], w[f"l{i}_conv_b"][None]]).reshape(4, 44, P)
                                .transpose(2, 1, 0).reshape(P, 176) for i in range(DEPTH)])
    ln_rows = np.stack([np.concatenate([w[f"l{i}_ln{j}_g"], w[f"l{i}_ln{j}_b"]]) for i in range(DEPTH) for j in (1, 2)])
    gn_cols = np.stack([w["l2_gn_g"], w["l2_gn_b"]]).reshape(2, 16, P).transpose(2, 1, 0).reshape(P, 32)
    arrays = {
        "x_rows": w["x"].reshape(SEQ, D),
        "x_cols": w["x"].reshape(SEQ, KD, P).transpose(2, 1, 0).reshape(P, KD * SEQ),
        "w_slots": lay_slots(w).reshape(N_SLOTS * P, SLOT),
        "ln_rows": ln_rows,
        "conv_cols": conv_cols,
        "gn_cols": gn_cols,
        "tables": tables.reshape(2 * P, TABLE),
        "consts": consts,
    }
    arrays = {k: np.ascontiguousarray(a) for k, a in arrays.items()}
    nc = bacc.Bacc("TRN2", target_bir_lowering=False, num_devices=1)
    args = [nc.dram_tensor(k, a.shape, F32, kind="ExternalInput").ap() for k, a in arrays.items()]
    out = nc.dram_tensor("y", (SEQ, D), F32, kind="ExternalOutput").ap()
    build(nc, *args, out, N_SUBS)
    return run(nc, [arrays], core_ids=[0]).results[0]["y"].reshape(1, SEQ, D)


N_SUBS = 2 * DEPTH
```

```python
from contextlib import ExitStack

import numpy as np

import concourse.bass as bass
from concourse import mybir

F32 = mybir.dt.float32
F32R = mybir.dt.float32r
ALU = mybir.AluOpType
ACT = mybir.ActivationFunctionType
AX_X = mybir.AxisListType.X

P = 128
SEQ = 256
TT = SEQ // P
D = 1024
KD = D // P
DEPTH = 4
ALPHA = (2 * DEPTH) ** 0.25
LN_EPS = 1e-5
GN_EPS = 1e-6
NEG = -1e30
TAKEN = -3e38
D_FF = 2816
STEPS = D_FF // 256
HEAD_DIM = 64
SCALE = HEAD_DIM ** -0.5
GROUPS = 4
TOPK = min(256, SEQ // 4)
IDX_HEADS = 8
IDX_SCALE = IDX_HEADS ** -0.5 * 64 ** -0.5
RET_HEADS = 4
SLOT = 2048
HALVES = 512
LOOP_ROUNDS = (STEPS - 5) // 2
VECTOR_PART = 1280
RING = 6
RAW = 3
TURNS = 4
MIXERS = ("dsa", "moba", "ret", "dsa")
TABLE = 1536
DSA_AHEAD = {("q", 0): 2, ("q", 1): 2, ("q", 2): 2, ("q", 3): 1, ("values", 0): 2, ("out", 0): 3}
WARM_BEFORE, WARM_BETWEEN, WARM_AFTER = (12, 6), 8, 2


def plan_sublayers():
    subs = []
    slot = turn = pair = 0

    def stage(out, name, g=0, slots=0, turns=0, pairs=0):
        nonlocal slot, turn, pair
        out.append((name, g, slot, turn, pair))
        slot += slots
        turn += turns
        pair += pairs

    for kind in MIXERS:
        s = []
        stage(s, "xT", 0, 0, 4 if subs else 0)
        if kind == "dsa":
            stage(s, "misc", 0, 1, 2)
            stage(s, "spread", 0, 0, 2)
            stage(s, "qi", 0, 1, 1)
            stage(s, "qi", 1, 1, 1)
            stage(s, "index", 0, 0, 3)
            stage(s, "index", 1, 0, 3)
            for g in range(GROUPS - 1):
                if g < 2:
                    stage(s, "topk", g)
                stage(s, "q", g, 1, 1)
            for g in range(GROUPS):
                stage(s, "scores", g, 0, 3)
                if g == 0:
                    stage(s, "q", GROUPS - 1, 1, 1)
                else:
                    stage(s, "out", g - 1, 1)
                stage(s, "probsT", g, 0, 3)
                stage(s, "values", g, 0, 1, 1)
            stage(s, "out", GROUPS - 1, 1)
        elif kind == "moba":
            stage(s, "mask")
            for n in "vkq":
                stage(s, n, 0, 1, 1)
            s.append(s.pop(-3))
            for g in range(GROUPS):
                stage(s, "scores", g, 0, 3)
                if g:
                    stage(s, "out", g - 1, 1)
                if g + 1 < GROUPS:
                    for n in "qkv":
                        stage(s, n, g + 1, 1, 1)
                stage(s, "probsT", g, 0, 3)
                stage(s, "values", g, 0, 1, 1)
            stage(s, "out", GROUPS - 1, 1)
        else:
            stage(s, "rv", 0, 1, 1)
            stage(s, "rv", 1, 1, 1)
            stage(s, "q", 0, 1, 1)
            stage(s, "k", 0, 1, 1)
            s[-4:] = s[-2:] + s[-4:-2]
            for h in range(RET_HEADS):
                if h:
                    stage(s, "rv", 2 * h, 1, 1)
                    stage(s, "rv", 2 * h + 1, 1, 1)
                stage(s, "rscores", h, 0, 1)
                if 0 < h < RET_HEADS - 1:
                    stage(s, "out", 2 * h - 2, 1)
                    stage(s, "out", 2 * h - 1, 1)
                stage(s, "rgate", 2 * h, 1, 1)
                stage(s, "rgate", 2 * h + 1, 1, 1)
                stage(s, "rvalues", h, 0, 2)
                if h + 1 < RET_HEADS:
                    stage(s, "q", h + 1, 1, 1)
                    stage(s, "k", h + 1, 1, 1)
                else:
                    stage(s, "out", 2 * h - 2, 1)
                stage(s, "ryT", h, 0, 2, 2)
            stage(s, "out", 2 * RET_HEADS - 3, 1)
            stage(s, "out", 2 * RET_HEADS - 2, 1)
            stage(s, "out", 2 * RET_HEADS - 1, 1)
        subs.append((kind, s))
        f = []
        stage(f, "xT", 0, 0, 4)
        stage(f, "ffn", 0, 3 * STEPS, 2 * STEPS, STEPS)
        subs.append(("ffn", f))
    return subs, slot, turn, pair


SUBS, N_SLOTS, N_TURNS, N_PAIRS = plan_sublayers()


def ffn_slots(first, s):
    up = first if s == 0 else first + 3 * s - 1 - (s == STEPS - 1)
    return up, up + 1, first + (3 * s + 4 if s < STEPS - 3 else 2 * STEPS + s)


def lay_slots(w):
    out = np.zeros((N_SLOTS, P, SLOT), np.float32)

    def up(n, m):
        out[n].reshape(P, KD, 256)[:, :, :m.shape[1]] = m.reshape(KD, P, -1).transpose(1, 0, 2)

    def down(n, m):
        out[n] = m.reshape(2, P, D).transpose(1, 0, 2).reshape(P, SLOT)

    def halves(first):
        c = first + np.arange(4 * HEAD_DIM).reshape(2, 2, 2, HEAD_DIM // 2)
        return c.transpose(0, 2, 1, 3).ravel()

    for i, kind in enumerate(MIXERS):
        w_in, w_out = w[f"l{i}_w_in"], w[f"l{i}_w_out"]
        seen = {}
        for name, g, n, _, _ in SUBS[2 * i][1]:
            if name == "out":
                down(n, w_out[256 * g:256 * g + 256])
            elif kind == "dsa" and name == "misc":
                up(n, w_in[:, np.r_[1024:1088, 1664:1728, 1088:1152, 1728:1736]])
            elif kind == "dsa" and name == "qi":
                up(n, w_in[:, halves(1152 + 256 * g)])
            elif kind in ("dsa", "moba") and name in ("q", "k"):
                up(n, w_in[:, halves((0 if name == "q" else D) + 256 * g)])
            elif kind == "moba" and name == "v":
                up(n, w_in[:, 2 * D + 256 * g:2 * D + 256 * g + 256])
            elif kind == "ret" and name in ("q", "k", "rv", "rgate"):
                c = {"q": 0, "k": D, "rv": 2 * D, "rgate": 4 * D}[name] + 256 * g
                up(n, w_in[:, c:c + 256])
        first = SUBS[2 * i + 1][1][1][2]
        w_up, w_down = w[f"l{i}_w_up"], w[f"l{i}_w_down"]
        for s in range(STEPS):
            a, b, c = ffn_slots(first, s)
            up(a, w_up[:, 256 * s:256 * s + 256])
            up(b, w_up[:, D_FF + 256 * s:D_FF + 256 * s + 256])
            down(c, w_down[256 * s:256 * s + 256])
    return out


def lay_tables():
    def rope(dim):
        inv = (1.0 / (np.float32(10000.0) ** (np.arange(0, dim, 2, dtype=np.float32) / np.float32(dim)))).astype(np.float32)
        ang = (np.arange(SEQ, dtype=np.float32)[None, :] * inv[:, None]).astype(np.float32)
        rep = P // (dim // 2)
        return np.tile(np.cos(ang), (rep, 1)), np.tile(np.sin(ang), (rep, 1))

    att = np.zeros((P, TABLE), np.float32)
    att[:, 0:256], att[:, 256:512] = rope(HEAD_DIM)
    att[64:P, 256:512] *= -1
    for i in range(2):
        for r in range(P):
            if r // 32 % 2 == i:
                att[r, 1024 + i] = 1.0
                for u in range(2):
                    att[64 * u + 32 * (r // 64) + r % 32, 512 + P * (2 * u + i) + r] = 1.0
    ret = np.zeros((P, TABLE), np.float32)
    ret[:, 0:256], ret[:, 256:512] = rope(2 * P)
    key, query = np.arange(P)[:, None], np.arange(P)[None, :]
    for h in range(RET_HEADS):
        log_gamma = np.log1p(-(2.0 ** (-5.0 - h)))
        diag = np.where(query >= key, np.exp((query - key) * log_gamma), 0.0)
        across = np.exp((P + query - key) * log_gamma)
        ret[:, 512 + 256 * h:640 + 256 * h] = diag / 16
        ret[:, 640 + 256 * h:768 + 256 * h] = across / 16
    ident = np.eye(P, dtype=np.float32)
    causal = np.zeros((P, 3 * P), np.float32)
    late = np.where(np.arange(P)[None, :] > np.arange(P)[:, None], np.float32(NEG), np.float32(0))
    causal[:, 0:P] = late
    causal[:, 2 * P:3 * P] = late
    return np.stack([att, ret]), np.concatenate([ident, causal], axis=1)


def build(nc, x_in, xT_in, w_slots, ln_rows, conv_cols, gn_cols, tables, consts, out, n_subs=2 * DEPTH):
    n_slots = N_SLOTS if n_subs == 2 * DEPTH else SUBS[n_subs][1][0][2]

    with ExitStack() as ctx:
        def sb(name, shape, dt=F32):
            return ctx.enter_context(nc.sbuf_tensor(name, shape, dt))

        def sem(name):
            return ctx.enter_context(nc.semaphore(name))

        raw = sb("raw", [P, RAW, SLOT])
        w_hi = sb("w_hi", [P, RING, SLOT], F32R)
        w_lo = sb("w_lo", [P, RING, SLOT], F32R)
        xT_hi = sb("xT_hi", [P, KD, SEQ], F32R)
        xT_lo = sb("xT_lo", [P, KD, SEQ], F32R)
        x = sb("x", [P, TT, D])
        ln = sb("ln", [P, 2, D])
        act_hi = sb("act_hi", [P, 2, 2, SEQ], F32R)
        act_lo = sb("act_lo", [P, 2, 2, SEQ], F32R)
        mask_r = sb("mask_r", [P, 3 * P], F32R)
        ident_r = sb("ident_r", [P, P], F32R)
        table = sb("table", [P, TABLE])
        const = sb("const", [P, 4 * P])
        conv = sb("conv", [P, 2 * D_FF // P, 4])
        gn = sb("gn", [P, 16, 2])
        stat = sb("stat", [P, 105])
        scratch = sb("scratch", [P, 8704])

        ident = const[:, 0:P]
        causal = const[:, P:4 * P]
        cos = table[:, 0:SEQ]
        sin = table[:, SEQ:2 * SEQ]

        def piece(at, *shape):
            size = int(np.prod(shape))
            v = scratch[:, at:at + size]
            if len(shape) == 2:
                return v.rearrange("p (a b) -> p a b", b=shape[1])
            if len(shape) == 3:
                return v.rearrange("p (a b c) -> p a b c", b=shape[1], c=shape[2])
            return v

        first_xT = piece(0, KD, SEQ)
        taps = [[piece(1024 * b + 512 * u, 2, SEQ) for u in range(2)] for b in range(2)]
        gate = [piece(2048 + 512 * b, 2, SEQ) for b in range(2)]
        prod = [piece(3072 + 512 * b, 2, SEQ) for b in range(2)]
        by_cos = piece(0, 2, SEQ)
        by_sin = piece(512, 2, SEQ)
        qT = [piece(1024 + 512 * g, 2, SEQ) for g in range(4)]
        k_diag = piece(3072, 2, 2, SEQ)
        v = [piece(4096 + 512 * g, TT, 256) for g in range(2)]
        probs = piece(5120, 1536)
        probsT = piece(6656, 1536)
        ki_diag = piece(5120, 2, SEQ)
        relu = [[piece(1024, 512), piece(1536, 512), piece(4608, 512)],
                [piece(7168, 512), piece(7680, 512), piece(8192, 512)]]
        index = piece(6144, 3 * P)
        left = piece(6528, 3 * P)
        narrow = piece(6912, SEQ)
        kT = [piece(3072 + 512 * g, 2, SEQ) for g in range(2)]
        ret_v = piece(4096, TT, 512)
        ret_gate = piece(5120, 4, SEQ)
        decayed = piece(6144, 3 * P)
        normed = piece(6656, TT, 512)
        scaled = [piece(2048 + 512 * b, 2, SEQ) for b in range(2)]
        ret_prod = [piece(7680 + 512 * b, 2, SEQ) for b in range(2)]

        acc = ctx.enter_context(nc.psum_tensor("acc", [P, TT, D], F32))
        work = ctx.enter_context(nc.psum_tensor("work", [P, TURNS, 512], F32))

        consts_in = sem("consts_in")
        gn_in = sem("gn_in")
        x_in_sem = sem("x_in_sem")
        xT_in_sem = sem("xT_in_sem")
        first_hi = sem("first_hi")
        first_lo = sem("first_lo")
        conv_in = sem("conv_in")
        ln_in = sem("ln_in")
        table_in = sem("table_in")
        raw_in = [sem(f"raw_in{r}") for r in range(RAW)]
        hi_ready = sem("hi_ready")
        lo_ready = sem("lo_ready")
        lo_end_ready = sem("lo_end_ready")
        turn_full = [sem(f"turn_full{b}") for b in range(TURNS)]
        turn_read = [sem(f"turn_read{b}") for b in range(TURNS)]
        xT_hi_ready = sem("xT_hi_ready")
        pair_prod = sem("pair_prod")
        pair_hi = sem("pair_hi")
        pair_lo = sem("pair_lo")
        pair_used = sem("pair_used")
        acc_bank = sem("acc_bank")
        first_tap = sem("first_tap")
        second_tap = sem("second_tap")
        gate_ready = sem("gate_ready")
        var_ready = sem("var_ready")
        std_ready = sem("std_ready")
        rstd_ready = sem("rstd_ready")
        tile0_scaled = sem("tile0_scaled")
        tile0_gained = sem("tile0_gained")
        x_ready = [sem(f"x_ready{t}") for t in range(TT)]
        ident_ready = sem("ident_ready")
        roped = sem("roped")
        keys_summed = sem("keys_summed")
        wi_ready = sem("wi_ready")
        mask_ready = sem("mask_ready")
        max_ready = sem("max_ready")
        probs_ready = sem("probs_ready")
        sums_inv = sem("sums_inv")
        dve_step = sem("dve_step")
        out_done = sem("out_done")

        def at(base, it, per):
            return base if it is None else it * per + base

        release = {}
        for si, (kind, stages) in enumerate(SUBS):
            outs = [st for st in stages if st[0] in ("values", "ryT")]
            first_pair = outs[0][4] if outs else 0
            for name, g, n, k, p in stages:
                if name in ("q", "k", "v", "qi", "rv", "rgate"):
                    release[n] = ("turn", k)
                elif name == "misc":
                    release[n] = ("turn", k + 1)
                elif name == "out":
                    release[n] = ("pair", first_pair + g)
                elif name == "ffn":
                    for s in range(STEPS):
                        a, b, c = ffn_slots(n, s)
                        release[a] = ("turn", k + 2 * s)
                        release[b] = ("turn", k + 2 * s + 1)
                        release[c] = ("pair", p + s)
        last_pair = {}
        product_pairs = []
        p_end = 0
        for si, (kind, stages) in enumerate(SUBS):
            for name, g, n, k, p in stages:
                made = {"values": 1, "ryT": 2, "ffn": STEPS}.get(name, 0)
                if name != "values":
                    product_pairs += range(p_end, p_end + made)
                p_end += made
            last_pair[si] = p_end

        last_slots = [SUBS[si + 1][1][0][2] - 1 if si + 1 < len(SUBS) else N_SLOTS - 1 for si in range(len(SUBS))]

        def products(p):
            return sum(1 for q in product_pairs if q <= p)

        def wait_full(eng, k, it=None):
            eng.wait_ge(turn_full[k % TURNS], at(k // TURNS + 1, it, 1))

        def wait_read(eng, k, it=None):
            eng.wait_ge(turn_read[k % TURNS], at(k // TURNS + 1, it, 1))

        def wait_slot_used(eng, n, it=None):
            what, i = release[n]
            if what == "turn":
                wait_full(eng, i, it)
            else:
                eng.wait_ge(pair_used, at(i + 1, it, 2))

        nth = {}
        ordinal = {}
        for si, (kind, stages) in enumerate(SUBS):
            for j, (name, g, n, k, p) in enumerate(stages):
                key = "rope" if name in ("q", "k", "qi", "spread") else name
                ordinal[si, j] = nth.get(key, 0)
                nth[key] = ordinal[si, j] + (2 if name == "spread" else 1)

        def dsa_count(si):
            return sum(1 for kind, _ in SUBS[:si + 1] if kind == "dsa")

        def mask_count(si):
            return sum(1 for kind, _ in SUBS[:si + 1] if kind in ("dsa", "moba"))

        def rope_needed(si, j):
            stages = SUBS[si][1]
            name, g = stages[j][:2]
            want = {"index": [("qi", g), ("spread", 0)], "scores": [("q", g), ("k", g), ("spread", 0)],
                    "rscores": [("q", g), ("k", g)]}[name]
            return max(ordinal[si, i] + (2 if st[0] == "spread" else 1)
                       for i, st in enumerate(stages) if (st[0], st[1]) in want)

        def find_turn(si, name, g):
            return next(st[3] for st in SUBS[si][1] if st[0] == name and st[1] == g)

        def v_turn(si, g):
            return find_turn(si, "misc", 0) + 1 if SUBS[si][0] == "dsa" else find_turn(si, "v", g)

        def rv_turn(si, g):
            return find_turn(si, "rv", g)

        def values_turn(si, g):
            return find_turn(si, "values", g)

        def var_count(what, si, g, t):
            n = sum(TT + (TT * RET_HEADS if kind == "ret" else 0) for kind, _ in SUBS[:si])
            if what == "ret":
                return n + TT * g + t + 1
            return n + (TT * RET_HEADS if SUBS[si][0] == "ret" else 0) + t + 1

        def ahead(si, j, full=False):
            name, g, n = SUBS[si][1][j][:3]
            first = SUBS[si][1][0][2]
            if n == last_slots[si] and not full:
                return n + 3
            if SUBS[si][0] == "dsa" and (name, g) in DSA_AHEAD:
                return n + DSA_AHEAD[name, g]
            starts = [i for i, st in enumerate(SUBS[si][1]) if first <= st[2] < first + {"moba": 3, "ret": 4}.get(SUBS[si][0], 0)
                      and st[0] in ("q", "k", "v", "rv")]
            return min(first + 3 + starts.index(j), first + RING - 1) if j in starts else n + 4

        def find_pair(si, h):
            return next(st[4] for st in SUBS[si][1] if st[0] == "ryT" and st[1] == h)

        subs = SUBS[:n_subs]
        block = ctx.enter_context(nc.Block())

        @block.sync
        def _(sp):
            sp.dma_start(first_xT[:, :, :].rearrange("p a b -> p (a b)"), xT_in).then_inc(xT_in_sem, 16)
            for n in range(RAW):
                sp.dma_start(raw[:, n, :], w_slots[n * P:(n + 1) * P, :]).then_inc(raw_in[n], 16)

            def load(n_here, row, r):
                sp.wait_ge(lo_ready, n_here)
                sp.wait_ge(lo_end_ready, n_here)
                sp.dma_start(raw[:, r, :], w_slots[row, :]).then_inc(raw_in[r], 16)

            rounds = n_slots // RAW - 1
            with sp.Fori(0, rounds) as it:
                for r in range(RAW):
                    load(it * RAW + (r + 1), bass.ds(it * (RAW * P) + (RAW + r) * P, P), r)
            for n in range(RAW * (rounds + 1), n_slots):
                load(n - RAW + 1, bass.ds(n * P, P), n % RAW)
            for t in range(TT):
                for half in range(2):
                    sp.wait_ge(x_ready[t], 2 * (n_subs - 1) + half + 1)
                    c = slice(512 * half, 512 * half + 512)
                    sp.dma_start(out[t * P:(t + 1) * P, c], x[:, t, c]).then_inc(out_done, 16)
            sp.wait_ge(out_done, 2 * 16 * TT)

        @block.tensor
        def _(pe):
            def mm(o, a, b, start, stop):
                return pe.matmul(o, a, b, start=start, stop=stop)

            def take_turn(k, it=None):
                if k >= TURNS or it is not None:
                    pe.wait_ge(turn_read[k % TURNS], at(k // TURNS, it, 1))

            def slot_in(n, it=None):
                pe.wait_ge(lo_ready, at(n + 1, it, RING))
                pe.wait_ge(lo_end_ready, at(n + 1, it, RING))

            def up_hi(n, k, a, b):
                return w_hi[:, n % RING, 256 * k + a:256 * k + b]

            def up_lo(n, k, a, b):
                return w_lo[:, n % RING, 256 * k + a:256 * k + b]

            def to_features(n, o, a, b, tok=slice(0, SEQ)):
                for k in range(KD):
                    mm(o, up_hi(n, k, a, b), xT_hi[:, k, tok], k == 0, False)
                    mm(o, up_hi(n, k, a, b), xT_lo[:, k, tok], False, False)
                    last = mm(o, up_lo(n, k, a, b), xT_hi[:, k, tok], False, k == KD - 1)
                return last

            def to_tokens(n, o, t, a, b):
                tok = slice(t * P, (t + 1) * P)
                for k in range(KD):
                    mm(o, xT_hi[:, k, tok], up_hi(n, k, a, b), k == 0, False)
                    mm(o, xT_hi[:, k, tok], up_lo(n, k, a, b), False, False)
                    last = mm(o, xT_lo[:, k, tok], up_hi(n, k, a, b), False, k == KD - 1)
                return last

            def project(n, k, it=None):
                slot_in(n, it)
                take_turn(k, it)
                for j in range(2):
                    last = to_features(n, work[:, k % TURNS, j * SEQ:(j + 1) * SEQ], j * P, (j + 1) * P)
                last.then_inc(turn_full[k % TURNS], 1)

            def token_slot(n, k, cols, tiles):
                if 0 in tiles:
                    slot_in(n)
                    take_turn(k)
                for t in tiles:
                    last = to_tokens(n, work[:, k % TURNS, 256 * t:256 * t + cols.stop - cols.start], t, cols.start, cols.stop)
                if TT - 1 in tiles:
                    last.then_inc(turn_full[k % TURNS], 1)

            def key_slot(n, k):
                take_turn(k)
                to_features(n, work[:, k % TURNS, 0:SEQ], 0, P).then_inc(turn_full[k % TURNS], 1)

            def keep_warm(o, n):
                for _ in range(n):
                    mm(o.rearrange("p (a b) -> p a b", b=P), ident_r[:, :],
                       ident_r[:, :].unsqueeze(1).to_broadcast([P, 4, P]), True, True)

            def transpose_tile(si, k, t):
                for half in range(2):
                    kk = k + 2 * t + half
                    take_turn(kk)
                    if t == 0:
                        keep_warm(work[:, kk % TURNS, :], WARM_BETWEEN if half else WARM_BEFORE[SUBS[si - 1][0] == "ffn"])
                    pe.wait_ge(x_ready[t], 2 * (si - 1) + half + 1)
                    for c in range(4):
                        f = (4 * half + c) * P
                        last = pe.transpose(work[:, kk % TURNS, c * P:(c + 1) * P], x[:, t, f:f + P], ident)
                    last.then_inc(turn_full[kk % TURNS], 1)

            def xT_in_place(k, t):
                wait_read(pe, k + 2 * t)
                wait_read(pe, k + 2 * t + 1)

            def start_sublayer(si, kind, stages):
                k = stages[0][3]
                if si == 0:
                    pe.wait_ge(first_lo, 2)
                    for cols, n, kk in early_slots(kind, stages):
                        token_slot(n, kk, cols, [0])
                    pe.wait_ge(consts_in, 16)
                    pe.wait_ge(ident_ready, 1)
                    return
                for t in range(TT):
                    transpose_tile(si, k, t)
                keep_warm(acc[:, 0, 0:HALVES], WARM_AFTER)
                xT_in_place(k, 0)
                if kind != "ffn":
                    for cols, n, kk in early_slots(kind, stages):
                        token_slot(n, kk, cols, [0])
                xT_in_place(k, 1)

            def early_slots(kind, stages):
                early = {"dsa": "misc", "moba": "v", "ret": "rv"}[kind]
                return [(slice(P, P + 72) if kind == "dsa" else slice(0, 256), n, k + (kind == "dsa"))
                        for name, g, n, k, _ in stages if name == early and g < (2 if kind == "ret" else 1)]

            def add_to_bank(n, p, t, half, j, start, stop):
                tok = slice(t * P, (t + 1) * P)
                hi, lo = act_hi[:, p % 2, j, tok], act_lo[:, p % 2, j, tok]
                c = j * D + half * HALVES
                wh = w_hi[:, n % RING, c:c + HALVES]
                wl = w_lo[:, n % RING, c:c + HALVES]
                o = acc[:, t, half * HALVES:(half + 1) * HALVES]
                mm(o, hi, wh, start, False)
                mm(o, hi, wl, False, False)
                return mm(o, lo, wh, False, stop)

            def accumulate(n, p, first, it=None):
                slot_in(n, it)
                for t in range(TT):
                    for j in range(2):
                        for half in range(2):
                            last = add_to_bank(n, p, t, half, j, first and j == 0, False)
                last.then_inc(pair_used, 1)

            def finish_one(n, p):
                slot_in(n)
                for t in range(TT):
                    for half in range(2):
                        for j in range(2):
                            last = add_to_bank(n, p, t, half, j, False, j == 1)
                        last.then_inc(*((pair_used, 1) if (t, half) == (1, 1) else (acc_bank, 1)))

            def finish_two(n, p, second_ready):
                slot_in(n)
                for half in range(2):
                    for j in range(2):
                        add_to_bank(n, p, 0, half, j, False, False)
                pe.wait_ge(pair_lo, second_ready)
                slot_in(n + 1)
                for half in range(2):
                    add_to_bank(n + 1, p + 1, 0, half, 0, False, False)
                    add_to_bank(n + 1, p + 1, 0, half, 1, False, True).then_inc(acc_bank, 1)
                for half in range(2):
                    add_to_bank(n, p, 1, half, 0, False, False)
                    last = add_to_bank(n, p, 1, half, 1, False, False)
                    if half == 1:
                        last.then_inc(pair_used, 1)
                    add_to_bank(n + 1, p + 1, 1, half, 0, False, False)
                    last = add_to_bank(n + 1, p + 1, 1, half, 1, False, True)
                    last.then_inc(*((acc_bank, 1) if half == 0 else (pair_used, 1)))

            def ffn(n0, k0, p0):
                def step(s, it=None):
                    a, b, _ = ffn_slots(n0, s)
                    project(a, k0 + 2 * s, it)
                    project(b, k0 + 2 * s + 1, it)
                    if 0 < s < STEPS - 2:
                        pe.wait_ge(pair_lo, at(products(p0 + s - 1), it, 2))
                        accumulate(b + 1, p0 + s - 1, s == 1, it)

                step(0)
                step(1)
                with pe.Fori(0, LOOP_ROUNDS) as it:
                    step(2, it)
                    step(3, it)
                for s in range(STEPS - 3, STEPS):
                    step(s)
                p = p0 + STEPS - 3
                pe.wait_ge(pair_lo, products(p))
                accumulate(ffn_slots(n0, STEPS - 3)[2], p, False)
                pe.wait_ge(pair_lo, products(p + 1))
                finish_two(ffn_slots(n0, STEPS - 2)[2], p + 1, products(p + 2))

            for si, (kind, stages) in enumerate(subs):
                for j, (name, g, n, k, p) in enumerate(stages):
                    if name == "xT":
                        start_sublayer(si, kind, stages)
                    elif name == "ffn":
                        ffn(n, k, p)
                    elif name == "misc":
                        key_slot(n, k)
                        token_slot(n, k + 1, slice(P, P + 72), [1])
                    elif name in ("q", "k", "qi", "rgate"):
                        project(n, k)
                    elif name in ("v", "rv"):
                        started = g < (2 if kind == "ret" else 1)
                        token_slot(n, k, slice(0, 256), [1] if started else [0, 1])
                    elif name == "spread":
                        wait_read(pe, k - 2)
                        pe.wait_ge(table_in, 16 * (si // 2 + 1))
                        for u in range(2):
                            take_turn(k + u)
                            for half in range(2):
                                sel = table[:, 512 + P * (2 * u + half):512 + P * (2 * u + half + 1)]
                                last = mm(work[:, (k + u) % TURNS, half * SEQ:(half + 1) * SEQ], sel, narrow, True, True)
                            last.then_inc(turn_full[(k + u) % TURNS], 1)
                    elif name in ("scores", "index"):
                        pe.wait_ge(roped, rope_needed(si, j))
                        if name == "scores":
                            pe.wait_ge(mask_ready, mask_count(si))
                            qs = qT[g if kind == "dsa" else g % 2]
                        else:
                            qs = qT[2 + g]
                        for part in range(3):
                            b = (k + part) % TURNS
                            take_turn(k + part)
                            keys = P if part == 0 else SEQ
                            heads = range(4) if part == 0 else range(2 * part - 2, 2 * part)
                            q0 = 0 if part == 0 else P
                            o = work[:, b, :].rearrange("p (h k) -> p h k", k=keys)
                            if name == "scores":
                                m = mask_r[:, 0:P] if part == 0 else mask_r[:, P:3 * P]
                                mm(o, ident_r[:, :], m.unsqueeze(1).to_broadcast([P, len(heads), keys]), True, False)
                            for u in ((0, 1) if part == 0 else (part - 1,)):
                                dst = o[:, 2 * u:2 * u + 2, :] if part == 0 else o
                                ks = ki_diag if name == "index" else k_diag[:, 0 if kind == "dsa" else u, :, :]
                                last = mm(dst, qs[:, u, q0:q0 + P], ks[:, :, 0:keys], name == "index",
                                          name == "index" or u == 1 or part > 0)
                            last.then_inc(turn_full[b], 1)
                    elif name == "probsT":
                        for part in range(3):
                            b = (k + part) % TURNS
                            take_turn(k + part)
                            pe.wait_ge(probs_ready, 3 * ordinal[si, j] + part + 1)
                            for c in range(4):
                                last = pe.transpose(work[:, b, c * P:(c + 1) * P],
                                                    probs[:, 512 * part + c * P:512 * part + (c + 1) * P], ident)
                            last.then_inc(turn_full[b], 1)
                    elif name == "values":
                        wait_read(pe, v_turn(si, g))
                        take_turn(k)
                        for part in range(3):
                            wait_read(pe, k - 3 + part)
                            for h in range(4) if part == 0 else range(2 * part - 2, 2 * part):
                                vh = v[0] if kind == "dsa" else v[g % 2][:, :, h * HEAD_DIM:(h + 1) * HEAD_DIM]
                                o = work[64 * (h % 2):64 * (h % 2) + 64, k % TURNS, :]
                                c0 = (h // 2) * SEQ
                                if part == 0:
                                    mm(o[:, c0:c0 + P], vh[:, 0, 0:HEAD_DIM], probsT[:, h * P:(h + 1) * P], True, True)
                                else:
                                    late = 512 + h * SEQ
                                    mm(o[:, c0 + P:c0 + SEQ], vh[:, 0, 0:HEAD_DIM], probsT[:, late:late + P], True, False)
                                    last = mm(o[:, c0 + P:c0 + SEQ], vh[:, 1, 0:HEAD_DIM], probsT[:, late + P:late + SEQ],
                                              False, True)
                        last.then_inc(turn_full[k % TURNS], 1)
                    elif name == "out":
                        _, pp = release[n]
                        if kind == "ret":
                            if n == last_slots[si]:
                                continue
                            pe.wait_ge(pair_lo, products(pp))
                            if n == last_slots[si] - 1:
                                finish_two(n, pp, products(pp + 1))
                            else:
                                accumulate(n, pp, g == 0)
                        elif n == last_slots[si]:
                            add_to_bank(n - 1, pp - 1, 1, 1, 0, False, False)
                            add_to_bank(n - 1, pp - 1, 1, 1, 1, False, False).then_inc(pair_used, 1)
                            wait_read(pe, values_turn(si, g))
                            finish_one(n, pp)
                        elif n == last_slots[si] - 1:
                            wait_read(pe, values_turn(si, g))
                            slot_in(n)
                            for t, half in ((0, 0), (0, 1), (1, 0)):
                                for chunk in range(2):
                                    add_to_bank(n, pp, t, half, chunk, False, False)
                        else:
                            wait_read(pe, values_turn(si, g))
                            accumulate(n, pp, g == 0)
                    elif name == "rscores":
                        pe.wait_ge(roped, rope_needed(si, j))
                        take_turn(k)
                        b = k % TURNS
                        for d in range(2):
                            mm(work[:, b, 0:SEQ], kT[g % 2][:, d, 0:P], qT[g % 2][:, d, :], d == 0, d == 1)
                        for d in range(2):
                            last = mm(work[:, b, SEQ:SEQ + P], kT[g % 2][:, d, P:SEQ], qT[g % 2][:, d, P:SEQ],
                                      d == 0, d == 1)
                        last.then_inc(turn_full[b], 1)
                    elif name == "rvalues":
                        wait_read(pe, find_turn(si, "rscores", g))
                        for u in range(2):
                            wait_read(pe, rv_turn(si, 2 * g + u))
                        take_turn(k)
                        mm(work[:, k % TURNS, :], decayed[:, 0:P], ret_v[:, 0, :], True, True)\
                            .then_inc(turn_full[k % TURNS], 1)
                        take_turn(k + 1)
                        o = work[:, (k + 1) % TURNS, :]
                        mm(o, decayed[:, P:2 * P], ret_v[:, 0, :], True, False)
                        mm(o, decayed[:, 2 * P:3 * P], ret_v[:, 1, :], False, True)\
                            .then_inc(turn_full[(k + 1) % TURNS], 1)
                    elif name == "ryT":
                        for t in range(TT):
                            wait_read(pe, find_turn(si, "rvalues", g) + t)
                        for u in range(2):
                            b = (k + u) % TURNS
                            take_turn(k + u)
                            for c in range(2):
                                for t in range(TT):
                                    f = (2 * u + c) * P
                                    last = pe.transpose(work[:, b, c * SEQ + t * P:c * SEQ + (t + 1) * P],
                                                        normed[:, t, f:f + P], ident)
                            last.then_inc(turn_full[b], 1)

        @block.scalar
        def _(act):
            fed = [0]

            def split_hi(n, it=None):
                act.wait_ge(raw_in[n % RAW], at(16 * (n // RAW + 1), it, 16 * (RING // RAW)))
                if n >= RING:
                    wait_slot_used(act, n - RING, it)
                act.activation(w_hi[:, n % RING, :], raw[:, n % RAW, :], ACT.Copy).then_inc(hi_ready, 1)

            def feed(upto):
                while fed[0] < min(upto + 1, n_slots):
                    split_hi(fed[0])
                    fed[0] += 1

            def ffn(n0, k0, p0, layer):
                def step(s, it=None):
                    a = ffn_slots(n0, s)[0]

                    def feed_one(i):
                        if it is not None:
                            split_hi(a + 3 + i, it)
                        else:
                            feed(a + i + (2 if s == 0 else 4 if s == STEPS - 1 else 3))

                    b = (p0 + s) % 2
                    for u in range(2):
                        k = k0 + 2 * s + u
                        if u == 0 and s >= 2:
                            act.wait_ge(pair_prod, at(products(p0 + s - 2), it, 2))
                        wait_full(act, k, it)
                        for j in range(2):
                            last = conv_col(b, u, j, k, s, it)
                        last.then_inc(first_tap, 1)
                        if s < STEPS - 1 or u == 0:
                            feed_one(u)
                    wait_read(act, k0 + 2 * s, it)
                    act.activation(gate[b][:, :, :], taps[b][0][:, :, :], ACT.Silu).then_inc(gate_ready, 1)
                    if s < STEPS - 1:
                        feed_one(2)
                    act.wait_ge(pair_prod, at(products(p0 + s), it, 2))
                    act.wait_ge(pair_used, at(p0 + s - 1, it, 2))
                    act.activation(act_hi[:, b, :, :], prod[b][:, :, :], ACT.Copy).then_inc(pair_hi, 1)
                    if s == STEPS - 1:
                        feed(last_slots[2 * layer + 1] + 3)

                def conv_col(b, u, j, k, s, it):
                    c = 2 * s + j + u * (D_FF // P)
                    if it is None:
                        w2, bias = conv[:, c, 2:3], conv[:, c, 3:4]
                    else:
                        w2 = conv[:, bass.ds(it * 4 + c, 1), 2:3].rearrange("p a b -> p (a b)")
                        bias = conv[:, bass.ds(it * 4 + c, 1), 3:4].rearrange("p a b -> p (a b)")
                    return act.activation(taps[b][u][:, j, :], work[:, k % TURNS, j * SEQ:(j + 1) * SEQ],
                                          ACT.Identity, bias=bias, scale=w2)

                act.wait_ge(conv_in, 16 * (layer + 1))
                step(0)
                step(1)
                with act.Fori(0, LOOP_ROUNDS) as it:
                    step(2, it)
                    step(3, it)
                fed[0] = ffn_slots(n0, STEPS - 3)[0] + 3
                for s in range(STEPS - 3, STEPS):
                    step(s)

            act.wait_ge(xT_in_sem, 16)
            for half in range(2):
                act.activation(xT_hi[:, 4 * half:4 * half + 4, :], first_xT[:, 4 * half:4 * half + 4, :], ACT.Copy)\
                    .then_inc(first_hi, 1)
            feed(0)
            act.wait_ge(consts_in, 16)
            act.activation(ident_r[:, :], ident, ACT.Copy).then_inc(ident_ready, 1)
            feed(3)
            for si, (kind, stages) in enumerate(subs):
                for j, (name, g, n, k, p) in enumerate(stages):
                    if name in ("q", "k", "qi", "v", "rv", "rgate", "misc", "out") or (kind, name, g) == ("dsa", "values", 0):
                        feed(ahead(si, j, True))
                    if name == "ffn":
                        ffn(n, k, p, si // 2)
                    elif name == "misc":
                        wait_full(act, k)
                        act.activation(narrow, work[:, k % TURNS, 0:SEQ], ACT.Copy).then_inc(turn_read[k % TURNS], 1)
                        wait_full(act, k + 1)
                        o = work[:, (k + 1) % TURNS, :].rearrange("p (t c) -> p t c", t=2)
                        act.activation(stat[:, 64:64 + 16].rearrange("p (t h) -> p t h", t=2), o[:, :, 64:72], ACT.Copy,
                                       scale=IDX_SCALE).then_inc(wi_ready, 1)
                        act.activation(v[0][:, :, 0:HEAD_DIM], o[:, :, 0:HEAD_DIM], ACT.Copy)\
                            .then_inc(turn_read[(k + 1) % TURNS], 1)
                    elif name in ("v", "rv"):
                        wait_full(act, k)
                        o = work[:, k % TURNS, :].rearrange("p (t c) -> p t c", t=2)
                        dst = v[g % 2][:, :, :] if name == "v" else ret_v[:, :, 256 * (g % 2):256 * (g % 2) + 256]
                        act.activation(dst, o, ACT.Copy).then_inc(turn_read[k % TURNS], 1)
                    elif name == "index":
                        for part in range(3):
                            wait_full(act, k + part)
                            act.activation(relu[g][part], work[:, (k + part) % TURNS, :], ACT.Relu)\
                                .then_inc(turn_read[(k + part) % TURNS], 1)
                    elif name == "scores":
                        o0 = ordinal[si, j]
                        if g:
                            wait_full(act, find_turn(si, "probsT", g - 1) + 2)
                        for part in range(3):
                            i = 3 * o0 + part
                            act.wait_ge(max_ready, i + 1)
                            keys = P if part == 0 else SEQ
                            heads = 4 if part == 0 else 2
                            c0 = 0 if part == 0 else 2 + 2 * part
                            for h in range(heads):
                                c = c0 + h
                                ins = act.activation(probs[:, 512 * part + h * keys:512 * part + (h + 1) * keys],
                                                     work[:, (k + part) % TURNS, h * keys:(h + 1) * keys], ACT.Exp,
                                                     bias=stat[:, 16 + c:17 + c], scale=SCALE,
                                                     accum_out=stat[:, 24 + c:25 + c])
                            ins.then_inc(turn_read[(k + part) % TURNS], 1)
                    elif name == "probsT":
                        if g:
                            wait_full(act, find_turn(si, "values", g - 1))
                        for part in (0, 2):
                            wait_full(act, k + part)
                            act.activation(probsT[:, 512 * part:512 * part + 512], work[:, (k + part) % TURNS, :], ACT.Copy)\
                                .then_inc(turn_read[(k + part) % TURNS], 1)
                    elif name == "values":
                        wait_full(act, k)
                        if p >= 2:
                            act.wait_ge(pair_used, p - 1)
                        act.activation(act_hi[:, p % 2, :, :], work[:, k % TURNS, :].rearrange("p (c t) -> p c t", c=2),
                                       ACT.Copy).then_inc(pair_hi, 1)
                    elif name == "rgate":
                        if g >= 2 and g % 2 == 0:
                            act.wait_ge(pair_prod, products(find_pair(si, g // 2 - 1) + 1))
                        wait_full(act, k)
                        act.activation(ret_gate[:, 2 * (g % 2):2 * (g % 2) + 2, :],
                                       work[:, k % TURNS, :].rearrange("p (c t) -> p c t", c=2), ACT.Silu)\
                            .then_inc(turn_read[k % TURNS], 1)
                    elif name == "rvalues":
                        for t in range(TT):
                            c = 2 * t
                            i = var_count("ret", si, g, t)
                            act.wait_ge(var_ready, i)
                            act.activation(stat[:, 80 + t:81 + t], stat[:, 40 + c + 1:42 + c], ACT.Sqrt,
                                           bias=stat[:, 101:102]).then_inc(std_ready, 1)
                    elif name == "ryT":
                        act.wait_ge(gn_in, 16)
                        for u in range(2):
                            wait_full(act, k + u)
                            pp = p + u
                            act.wait_ge(pair_prod, products(pp - 2))
                            for c in range(2):
                                col = 4 * g + 2 * u + c
                                ins = act.activation(scaled[u][:, c, :], work[:, (k + u) % TURNS, c * SEQ:(c + 1) * SEQ],
                                                     ACT.Identity, bias=gn[:, col, 1:2], scale=gn[:, col, 0:1])
                            ins.then_inc(turn_read[(k + u) % TURNS], 1)
                        for u in range(2):
                            pp = p + u
                            act.wait_ge(pair_prod, products(pp))
                            act.wait_ge(pair_used, pp - 1)
                            act.activation(act_hi[:, pp % 2, :, :], ret_prod[u][:, :, :], ACT.Copy).then_inc(pair_hi, 1)
                act.activation(stat[:, 102:103], stat[:, 100:101], ACT.Sqrt)
                for t in range(TT):
                    act.wait_ge(var_ready, var_count("ln", si, 0, t))
                    act.activation(stat[:, 4 + t:5 + t], stat[:, 2 * t + 1:2 * t + 2], ACT.Sqrt,
                                   bias=stat[:, 100:101]).then_inc(std_ready, 1)
                    if t == 0:
                        act.wait_ge(rstd_ready, si + 1)
                        for half in range(2):
                            c = slice(512 * half, 512 * half + 512)
                            act.activation(x[:, 0, c], x[:, 0, c], ACT.Identity, bias=stat[:, 104 - half:105 - half],
                                           scale=stat[:, 6:7]).then_inc(tile0_scaled, 1)
                if si + 1 < n_subs:
                    for i in range(2 * TT):
                        t, half = i // 2, i % 2
                        kk = SUBS[si + 1][1][0][3] + i
                        wait_full(act, kk)
                        act.activation(xT_hi[:, 4 * half:4 * half + 4, t * P:(t + 1) * P],
                                       work[:, kk % TURNS, :].rearrange("p (c t) -> p c t", c=4), ACT.Copy)\
                            .then_inc(xT_hi_ready, 1)

        @block.vector
        def _(dve):
            fed = [0]
            steps = [0]

            def mark(ins):
                steps[0] += 1
                ins.then_inc(dve_step, 1)
                return steps[0]

            def settle(ins):
                dve.wait_ge(dve_step, mark(ins))

            def split_lo(n, it=None):
                dve.wait_ge(hi_ready, at(n + 1, it, RING))
                c = slice(0, VECTOR_PART)
                dve.tensor_tensor(w_lo[:, n % RING, c], raw[:, n % RAW, c], w_hi[:, n % RING, c], ALU.subtract)\
                    .then_inc(lo_ready, 1)

            def feed(upto):
                while fed[0] < min(upto + 1, n_slots):
                    split_lo(fed[0])
                    fed[0] += 1

            def ffn(n0, k0, p0, layer):
                def col(s, u, j, tap, it):
                    c = 2 * s + j + u * (D_FF // P)
                    if it is None:
                        return conv[:, c, tap:tap + 1]
                    return conv[:, bass.ds(it * 4 + c, 1), tap:tap + 1].rearrange("p a b -> p (a b)")

                def step(s, it=None):
                    a = ffn_slots(n0, s)[0]
                    b = (p0 + s) % 2

                    def feed_one(i):
                        if it is not None:
                            split_lo(a + 3 + i, it)
                        else:
                            feed(a + i + (2 if s == 0 else 4 if s == STEPS - 1 else 3))

                    for u in range(2):
                        k = k0 + 2 * s + u
                        i = 2 * (STEPS * layer + s) + u
                        dve.wait_ge(first_tap, at(i + 1, it, 4))
                        for j in range(2):
                            o, h = taps[b][u][:, j, :], work[:, k % TURNS, j * SEQ:(j + 1) * SEQ]
                            ins = dve.scalar_tensor_tensor(out=o[:, 1:SEQ], in0=h[:, 0:SEQ - 1], scalar=col(s, u, j, 1, it),
                                                           in1=o[:, 1:SEQ], op0=ALU.mult, op1=ALU.add)
                        ins.then_inc(second_tap, 1)
                        dve.wait_ge(second_tap, at(i + 1, it, 4))
                        for j in range(2):
                            o, h = taps[b][u][:, j, :], work[:, k % TURNS, j * SEQ:(j + 1) * SEQ]
                            ins = dve.scalar_tensor_tensor(out=o[:, 2:SEQ], in0=h[:, 0:SEQ - 2], scalar=col(s, u, j, 0, it),
                                                           in1=o[:, 2:SEQ], op0=ALU.mult, op1=ALU.add)
                        ins.then_inc(turn_read[k % TURNS], 1)
                        if s < STEPS - 1 or u == 0:
                            feed_one(u)
                    if s < STEPS - 1:
                        feed_one(2)
                    dve.wait_ge(gate_ready, at(STEPS * layer + s + 1, it, 2))
                    wait_read(dve, k0 + 2 * s + 1, it)
                    dve.wait_ge(pair_lo, at(products(p0 + s - 2), it, 2)) if products(p0 + s - 2) else None
                    dve.tensor_tensor(prod[b][:, :, :], gate[b][:, :, :], taps[b][1][:, :, :], ALU.mult)\
                        .then_inc(pair_prod, 1)
                    if s == STEPS - 1:
                        feed(last_slots[2 * layer + 1] + 1)

                step(0)
                step(1)
                with dve.Fori(0, LOOP_ROUNDS) as it:
                    step(2, it)
                    step(3, it)
                fed[0] = ffn_slots(n0, STEPS - 3)[0] + 3
                for s in range(STEPS - 3, STEPS):
                    step(s)

            def norm(si, last_slot):
                def cols(h):
                    return slice(512 * h, 512 * h + 512)

                def add_residual(t, h):
                    if (t, h) == (1, 1):
                        dve.wait_ge(pair_used, last_pair[si])
                    else:
                        dve.wait_ge(acc_bank, 3 * si + 2 * t + h + 1)
                    return mark(dve.scalar_tensor_tensor(out=x[:, t, cols(h)], in0=x[:, t, cols(h)], scalar=float(ALPHA),
                                                         in1=acc[:, t, cols(h)], op0=ALU.mult, op1=ALU.add))

                def stats(t, h, added):
                    dve.wait_ge(dve_step, added)
                    return mark(dve.bn_stats(stat[:, 48 + 6 * h:54 + 6 * h], x[:, t, cols(h)]))

                def mean_and_variance(t, counted):
                    dve.wait_ge(dve_step, counted)
                    dve.bn_aggr(stat[:, 2 * t:2 * t + 2], stat[:, 48:60]).then_inc(var_ready, 1)

                def times_gain(t, c):
                    dve.wait_ge(var_ready, var_count("ln", si, 0, t))
                    return mark(dve.scalar_tensor_tensor(out=x[:, t, c], in0=x[:, t, c], scalar=stat[:, 2 * t:2 * t + 1],
                                                         in1=ln[:, 0, c], op0=ALU.subtract, op1=ALU.mult))

                def inverse(t):
                    dve.wait_ge(std_ready, var_count("ln", si, 0, t))
                    return dve.reciprocal(stat[:, 6 + t:7 + t], stat[:, 4 + t:5 + t])

                dve.wait_ge(ln_in, 16 * (si + 1))
                if si == 0:
                    dve.wait_ge(x_in_sem, 16 * TT)
                stats(0, 0, add_residual(0, 0))
                mean_and_variance(0, stats(0, 1, add_residual(0, 1)))
                added = add_residual(1, 0)
                inverted = mark(inverse(0))
                gained = times_gain(0, cols(0))
                dve.wait_ge(dve_step, inverted)
                dve.tensor_scalar(stat[:, 103:104], stat[:, 0:1], stat[:, 6:7], -1.0, ALU.mult, ALU.mult)\
                    .then_inc(rstd_ready, 1)
                dve.wait_ge(dve_step, gained)
                stats(1, 0, added)
                mean_and_variance(1, stats(1, 1, add_residual(1, 1)))
                times_gain(1, slice(0, D))
                settle(inverse(1))
                for h in range(2):
                    dve.scalar_tensor_tensor(out=x[:, 1, cols(h)], in0=x[:, 1, cols(h)], scalar=stat[:, 7:8],
                                             in1=ln[:, 1, cols(h)], op0=ALU.mult, op1=ALU.add).then_inc(x_ready[1], 1)
                if si + 1 < n_subs:
                    for t in range(TT):
                        for half in range(2):
                            kk = SUBS[si + 1][1][0][3] + 2 * t + half
                            dve.wait_ge(xT_hi_ready, 4 * si + 2 * t + half + 1)
                            dst = (slice(None), slice(4 * half, 4 * half + 4), slice(t * P, (t + 1) * P))
                            dve.tensor_tensor(xT_lo[dst], work[:, kk % TURNS, :].rearrange("p (c t) -> p c t", c=4),
                                              xT_hi[dst], ALU.subtract).then_inc(turn_read[kk % TURNS], 1)
                    feed(last_slot + (3 if SUBS[si][0] == "ffn" else 4))

            def rotate(k, r, table_n, in_rows):
                wait_full(dve, k)
                dve.wait_ge(table_in, 16 * table_n)
                if r:
                    dve.wait_ge(roped, r)
                src = work[:, k % TURNS, :].rearrange("p (c t) -> p c t", c=2)
                dve.tensor_tensor(by_cos[:, :, :], src, cos.unsqueeze(1).to_broadcast([P, 2, SEQ]), ALU.mult)
                for to, rows in ((64, slice(0, 64)), (0, slice(64, P))) if in_rows else ((0, slice(0, P)),):
                    last = dve.tensor_tensor(by_sin[to:to + (rows.stop - rows.start), :, :], src[rows, :, :],
                                             sin[rows, :].unsqueeze(1).to_broadcast([rows.stop - rows.start, 2, SEQ]), ALU.mult)
                last.then_inc(turn_read[k % TURNS], 1)

            def topk(rounds):
                tiles = ((0, P), (P, 3 * P))
                taken = [0, 0]
                for r in rounds:
                    src = index if r == 0 else left
                    found = [0, 0]
                    for t, (a, b) in enumerate(tiles):
                        if taken[t]:
                            dve.wait_ge(dve_step, taken[t])
                        found[t] = mark(dve.max(stat[:, 84 + 8 * t:92 + 8 * t], src[:, a:b]))
                    for t, (a, b) in enumerate(tiles):
                        dve.wait_ge(dve_step, found[t])
                        taken[t] = mark(dve.match_replace(left[:, a:b], stat[:, 84 + 8 * t:92 + 8 * t], src[:, a:b], TAKEN))
                dve.wait_ge(dve_step, steps[0])

            dve.memset(stat[:, 100:101], LN_EPS)
            dve.memset(stat[:, 104:105], 0.0)
            settle(dve.memset(stat[:, 101:102], GN_EPS))
            for half in range(2):
                c = slice(4 * half, 4 * half + 4)
                dve.wait_ge(first_hi, half + 1)
                dve.tensor_tensor(xT_lo[:, c, :], first_xT[:, c, :], xT_hi[:, c, :], ALU.subtract).then_inc(first_lo, 1)
            feed(3)
            dve.wait_ge(consts_in, 16)
            for si, (kind, stages) in enumerate(subs):
                for j, (name, g, n, k, p) in enumerate(stages):
                    if name in ("q", "k", "qi", "v", "rv", "rgate", "misc", "out") or (kind, name, g) == ("dsa", "values", 0):
                        feed(ahead(si, j))
                    if name == "ffn":
                        ffn(n, k, p, si // 2)
                    elif name == "spread":
                        for u in range(2):
                            rotate(k + u, ordinal[si, j] + u, si // 2 + 1, True)
                    elif name in ("q", "k", "qi"):
                        rotate(k, ordinal[si, j], si // 2 + 1, kind != "ret")
                    elif name == "index":
                        if g == 0:
                            dve.wait_ge(wi_ready, dsa_count(si))
                        order = [(0, 0, 0), (1, 1, 0), (0, 0, 1), (1, 1, 1), (0, 0, 2), (1, 2, 2), (0, 0, 3), (1, 2, 3)]
                        summed = [steps[0], steps[0]]
                        for t, part, h in order:
                            keys = (t + 1) * P
                            m = h if t == 0 else h % 2
                            wait_read(dve, k + part)
                            dve.wait_ge(dve_step, summed[t])
                            dst = index[:, P * t:P * t + keys]
                            base = causal[:, P * t:P * t + keys] if (g, h) == (0, 0) else dst
                            summed[t] = mark(dve.scalar_tensor_tensor(
                                out=dst, in0=relu[g][part][:, m * keys:(m + 1) * keys],
                                scalar=stat[:, 64 + 8 * t + 4 * g + h:65 + 8 * t + 4 * g + h],
                                in1=base, op0=ALU.mult, op1=ALU.add))
                        dve.wait_ge(dve_step, steps[0])
                    elif name == "topk":
                        half = TOPK // 16
                        topk(range(half * g, half * g + half))
                        if g == 1:
                            settle(dve.tensor_scalar(index, left, TAKEN / 2, NEG, ALU.is_ge, ALU.mult))
                            dve.tensor_tensor(mask_r[:, :], index, causal, ALU.add).then_inc(mask_ready, 1)
                    elif name == "mask":
                        dve.tensor_copy(mask_r[:, :], causal).then_inc(mask_ready, 1)
                    elif name == "scores":
                        for part in range(3):
                            wait_full(dve, k + part)
                            keys = P if part == 0 else SEQ
                            heads = 4 if part == 0 else 2
                            c0 = 0 if part == 0 else 2 + 2 * part
                            settle(dve.tensor_reduce(stat[:, 8 + c0:8 + c0 + heads],
                                                     work[:, (k + part) % TURNS, :].rearrange("p (h k) -> p h k", k=keys),
                                                     AX_X, ALU.max))
                            dve.tensor_scalar(stat[:, 16 + c0:16 + c0 + heads], stat[:, 8 + c0:8 + c0 + heads],
                                              -SCALE, None, ALU.mult).then_inc(max_ready, 1)
                        for part in range(3):
                            wait_read(dve, k + part)
                            heads = 4 if part == 0 else 2
                            c0 = 0 if part == 0 else 2 + 2 * part
                            dve.reciprocal(stat[:, 32 + c0:32 + c0 + heads], stat[:, 24 + c0:24 + c0 + heads])\
                                .then_inc(sums_inv, 1)
                    elif name == "probsT":
                        wait_full(dve, k + 1)
                        if g:
                            wait_full(dve, find_turn(si, "values", g - 1))
                        dve.tensor_copy(probsT[:, 512:1024], work[:, (k + 1) % TURNS, :])\
                            .then_inc(turn_read[(k + 1) % TURNS], 1)
                    elif name == "values":
                        dve.wait_ge(pair_hi, p + 1)
                        dve.tensor_tensor(act_lo[:, p % 2, :, :], work[:, k % TURNS, :].rearrange("p (c t) -> p c t", c=2),
                                          act_hi[:, p % 2, :, :], ALU.subtract).then_inc(turn_read[k % TURNS], 1)
                    elif name == "rscores":
                        wait_full(dve, k)
                        o = work[:, k % TURNS, :]
                        d0 = 512 + 256 * g
                        dve.tensor_tensor(decayed[:, 0:SEQ], o[:, 0:SEQ], table[:, d0:d0 + SEQ], ALU.mult)
                        dve.tensor_tensor(decayed[:, SEQ:SEQ + P], o[:, SEQ:SEQ + P], table[:, d0:d0 + P], ALU.mult)\
                            .then_inc(turn_read[k % TURNS], 1)
                    elif name == "rvalues":
                        for t in range(TT):
                            o = work[:, (k + t) % TURNS, :]
                            wait_full(dve, k + t)
                            settle(dve.bn_stats(stat[:, 48 + 6 * t:54 + 6 * t], o))
                            dve.bn_aggr(stat[:, 40 + 2 * t:42 + 2 * t], stat[:, 48 + 6 * t:54 + 6 * t]).then_inc(var_ready, 1)
                        if g:
                            wait_full(dve, find_turn(si, "ryT", g - 1) + 1)
                        for t in range(TT):
                            o = work[:, (k + t) % TURNS, :]
                            dve.wait_ge(std_ready, var_count("ret", si, g, t))
                            settle(dve.reciprocal(stat[:, 82 + t:83 + t], stat[:, 80 + t:81 + t]))
                            dve.tensor_scalar(normed[:, t, :], o, stat[:, 40 + 2 * t:41 + 2 * t], stat[:, 82 + t:83 + t],
                                              ALU.subtract, ALU.mult).then_inc(turn_read[(k + t) % TURNS], 1)
                    elif name == "ryT":
                        for u in range(2):
                            pp = p + u
                            wait_read(dve, k + u)
                            dve.wait_ge(pair_lo, products(pp - 2))
                            dve.tensor_tensor(ret_prod[u][:, :, :], scaled[u][:, :, :], ret_gate[:, 2 * u:2 * u + 2, :],
                                              ALU.mult).then_inc(pair_prod, 1)
                norm(si, last_slots[si])

        @block.gpsimd
        def _(pool):
            def load_ln(si):
                pool.dma_start(ln[:, :, :].rearrange("p a d -> p (a d)"), ln_rows[si, :].partition_broadcast(P))\
                    .then_inc(ln_in, 16)

            def load_table(i):
                pool.dma_start(table[:, :], tables[P * (MIXERS[i] == "ret"):P * (MIXERS[i] == "ret") + P, :])\
                    .then_inc(table_in, 16)

            def load_conv(i):
                pool.dma_start(conv[:, :, :].rearrange("p a b -> p (a b)"), conv_cols[P * i:P * (i + 1), :])\
                    .then_inc(conv_in, 16)

            fed = [0]

            def split_end(n, it=None):
                pool.wait_ge(hi_ready, at(n + 1, it, RING))
                c = slice(VECTOR_PART, SLOT)
                pool.tensor_tensor(w_lo[:, n % RING, c], raw[:, n % RAW, c], w_hi[:, n % RING, c], ALU.subtract)\
                    .then_inc(lo_end_ready, 1)

            def feed(upto):
                while fed[0] < min(upto + 1, n_slots):
                    split_end(fed[0])
                    fed[0] += 1

            def rest(p, src, it=None):
                pool.wait_ge(pair_hi, at(p + 1, it, 2))
                pool.tensor_tensor(act_lo[:, p % 2, :, :], src[:, :, :], act_hi[:, p % 2, :, :], ALU.subtract)\
                    .then_inc(pair_lo, 1)

            pool.dma_start(const[:, :], consts).then_inc(consts_in, 16)
            pool.wait_ge(raw_in[0], 16)
            load_table(0)
            feed(3)
            load_conv(0)
            for t in range(TT):
                pool.dma_start(x[:, t, :], x_in[t * P:(t + 1) * P, :]).then_inc(x_in_sem, 16)
            load_ln(0)
            pool.dma_start(gn[:, :, :].rearrange("p a b -> p (a b)"), gn_cols).then_inc(gn_in, 16)

            for si, (kind, stages) in enumerate(subs):
                for j, (name, g, n, k, p) in enumerate(stages):
                    if name in ("q", "k", "qi", "v", "rv", "rgate", "misc", "out") or (kind, name, g) == ("dsa", "values", 0):
                        feed(ahead(si, j))
                    if name in ("q", "k", "qi", "spread"):
                        for u in range(2 if name == "spread" else 1):
                            wait_read(pool, k + u)
                            if kind == "ret":
                                dst = (kT if name == "k" else qT)[g % 2]
                                pool.tensor_tensor(dst[:, 0, :], by_cos[:, 0, :], by_sin[:, 1, :], ALU.subtract)
                                last = pool.tensor_tensor(dst[:, 1, :], by_cos[:, 1, :], by_sin[:, 0, :], ALU.add)
                            elif name == "k":
                                pool.tensor_tensor(by_cos[:, :, :], by_cos[:, :, :], by_sin[:, :, :], ALU.add)\
                                    .then_inc(keys_summed, 1)
                                pool.wait_ge(keys_summed, g + 1)
                                for i in range(2):
                                    block = table[:, 1024 + i:1025 + i].unsqueeze(1).to_broadcast([P, 2, SEQ])
                                    last = pool.tensor_tensor(k_diag[:, :, i, :], by_cos[:, :, :], block, ALU.mult)
                            else:
                                dst = (k_diag[:, 0, :, :], ki_diag)[u] if name == "spread" else \
                                    qT[2 + g] if name == "qi" else qT[g if kind == "dsa" else g % 2]
                                last = pool.tensor_tensor(dst[:, :, :], by_cos[:, :, :], by_sin[:, :, :], ALU.add)
                            last.then_inc(roped, 1)
                    elif name == "scores":
                        for part in range(3):
                            i = 3 * ordinal[si, j] + part
                            keys = P if part == 0 else SEQ
                            heads = 4 if part == 0 else 2
                            c0 = 0 if part == 0 else 2 + 2 * part
                            pool.wait_ge(sums_inv, i + 1)
                            pr = probs[:, 512 * part:512 * part + 512].rearrange("p (h k) -> p h k", k=keys)
                            pool.tensor_tensor(pr, pr, stat[:, 32 + c0:32 + c0 + heads].unsqueeze(2)
                                               .to_broadcast([P, heads, keys]), ALU.mult).then_inc(probs_ready, 1)
                    elif name == "ryT":
                        for u in range(2):
                            rest(p + u, ret_prod[u])
                    elif name == "ffn":
                        for s in range(2):
                            feed(ffn_slots(n, s)[0] + (5 if s else 4))
                            rest(p + s, prod[(p + s) % 2])
                        with pool.Fori(0, LOOP_ROUNDS) as it:
                            for s in (2, 3):
                                for i in range(3):
                                    split_end(ffn_slots(n, s)[0] + 3 + i, it)
                                rest(p + s, prod[(p + s) % 2], it)
                        fed[0] = ffn_slots(n, STEPS - 3)[0] + 3
                        for s in range(STEPS - 3, STEPS):
                            feed(ffn_slots(n, s)[0] + (5 if s < STEPS - 1 else 4))
                            rest(p + s, prod[(p + s) % 2])
                        feed(last_slots[si] + 2)
                c0, c1 = slice(0, 512), slice(512, D)
                pool.wait_ge(tile0_scaled, 2 * si + 1)
                pool.tensor_tensor(x[:, 0, c0], x[:, 0, c0], ln[:, 1, c0], ALU.add).then_inc(x_ready[0], 1)
                pool.wait_ge(tile0_scaled, 2 * si + 2)
                pool.tensor_tensor(x[:, 0, c1], x[:, 0, c1], ln[:, 0, c1], ALU.mult).then_inc(tile0_gained, 1)
                pool.wait_ge(tile0_gained, si + 1)
                pool.tensor_tensor(x[:, 0, c1], x[:, 0, c1], ln[:, 1, c1], ALU.add).then_inc(x_ready[0], 1)
                if si + 1 < n_subs:
                    for t in range(TT):
                        pool.wait_ge(x_ready[t], 2 * (si + 1))
                    load_ln(si + 1)
                    if si % 2:
                        load_conv(si // 2 + 1)
                    elif si // 2 + 1 < DEPTH:
                        load_table(si // 2 + 1)


def kernel(**inputs):
    import concourse.bacc as bacc
    from concourse.bass_utils import run_bass_kernel_spmd as run

    w = {k: np.asarray(a) for k, a in inputs.items()}
    tables, consts = lay_tables()
    conv_cols = np.concatenate([np.concatenate([w[f"l{i}_conv_w"], w[f"l{i}_conv_b"][None]]).reshape(4, 44, P)
                                .transpose(2, 1, 0).reshape(P, 176) for i in range(DEPTH)])
    ln_rows = np.stack([np.concatenate([w[f"l{i}_ln{j}_g"], w[f"l{i}_ln{j}_b"]]) for i in range(DEPTH) for j in (1, 2)])
    gn_cols = np.stack([w["l2_gn_g"], w["l2_gn_b"]]).reshape(2, 16, P).transpose(2, 1, 0).reshape(P, 32)
    arrays = {
        "x_rows": w["x"].reshape(SEQ, D),
        "x_cols": w["x"].reshape(SEQ, KD, P).transpose(2, 1, 0).reshape(P, KD * SEQ),
        "w_slots": lay_slots(w).reshape(N_SLOTS * P, SLOT),
        "ln_rows": ln_rows,
        "conv_cols": conv_cols,
        "gn_cols": gn_cols,
        "tables": tables.reshape(2 * P, TABLE),
        "consts": consts,
    }
    arrays = {k: np.ascontiguousarray(a) for k, a in arrays.items()}
    nc = bacc.Bacc("TRN2", target_bir_lowering=False, num_devices=1)
    args = [nc.dram_tensor(k, a.shape, F32, kind="ExternalInput").ap() for k, a in arrays.items()]
    out = nc.dram_tensor("y", (SEQ, D), F32, kind="ExternalOutput").ap()
    build(nc, *args, out, N_SUBS)
    return run(nc, [arrays], core_ids=[0]).results[0]["y"].reshape(1, SEQ, D)


N_SUBS = 2 * DEPTH
```
